# Optimizing a Trainium2 kernel written in Bass

```python
import math
import jax, jax.numpy as jnp
from jax import lax
import numpy as np

D_MODEL = 1024
BATCH = 1
SEQ = 1024
DEPTH = 1

CHUNK = 64
MIX_WIDTH = D_MODEL
ATTN_WIDTH = MIX_WIDTH // 2
SSM_WIDTH = MIX_WIDTH - ATTN_WIDTH
HEAD_DIM = 64
N_HEADS = ATTN_WIDTH // HEAD_DIM
Q_BLOCK = 128
SSM_GROUP = 16
N_SSM_GROUPS = SSM_WIDTH // SSM_GROUP
SSM_STATE = 64
DT_MIN = 1e-3
DT_MAX = 1e-1
IN_WIDTH = 3 * ATTN_WIDTH + N_HEADS + SSM_WIDTH
N_EXPERTS = 32
TOP_K = 4
D_FF = D_MODEL
SWIGLU_LIMIT = 7.0
SWIGLU_ALPHA = 1.702
MOE_BLOCK = 128
PLE_DIM = 256
NORM_EPS = 1e-5

kernel_name = "hymba_s5_fox_moe_ple_encoder"

def rmsnorm(x, g):
    xf = x.astype(jnp.float32)
    y = xf * lax.rsqrt(jnp.mean(xf * xf, axis=-1, keepdims=True) + NORM_EPS)
    return (y * g.astype(jnp.float32)).astype(x.dtype)

def forgetting_attention(q, k, v, log_f):
    b, s, h, dh = q.shape
    n_blk = s // Q_BLOCK
    c_t = jnp.cumsum(log_f, axis=1).transpose(0, 2, 1)
    c_blocks = c_t.reshape(b, h, n_blk, Q_BLOCK).transpose(2, 0, 1, 3)
    q_blocks = q.reshape(b, n_blk, Q_BLOCK, h, dh).transpose(1, 0, 2, 3, 4)
    key_pos = jnp.arange(s)
    scale = dh ** -0.5

    def one_block(args):
        i, q_i, c_i = args
        q_pos = i * Q_BLOCK + jnp.arange(Q_BLOCK)
        logits = jnp.einsum('bqhd,bkhd->bhqk', q_i, k,
                            preferred_element_type=jnp.float32) * scale
        logits = logits + c_i[..., :, None] - c_t[..., None, :]
        logits = jnp.where(key_pos[None, :] <= q_pos[:, None], logits, -jnp.inf)
        w = jax.nn.softmax(logits, axis=-1)
        return jnp.einsum('bhqk,bkhd->bqhd', w.astype(v.dtype), v)

    out = lax.map(one_block, (jnp.arange(n_blk), q_blocks, c_blocks))
    return out.transpose(1, 0, 2, 3, 4).reshape(b, s, h, dh)

def s5_mixer(u, lam_re, lam_im, log_dt, b_re, b_im, c_re, c_im, d_skip, w_glu, b_glu):
    bsz, s, _ = u.shape
    f32 = jnp.float32
    uf = u.astype(f32).reshape(bsz, s, N_SSM_GROUPS, SSM_GROUP)
    dt = jnp.exp(log_dt.astype(f32))[:, None]
    lr = lam_re.astype(f32)
    li = lam_im.astype(f32)
    mag = jnp.exp(lr * dt)
    ab_re = mag * jnp.cos(li * dt)
    ab_im = mag * jnp.sin(li * dt)
    den = lr * lr + li * li
    nr = ab_re - 1.0
    z_re = (nr * lr + ab_im * li) / den
    z_im = (ab_im * lr - nr * li) / den
    br = b_re.astype(f32)
    bi = b_im.astype(f32)
    bb_re = z_re[..., None] * br - z_im[..., None] * bi
    bb_im = z_re[..., None] * bi + z_im[..., None] * br
    bu_re = jnp.einsum('bsgc,gpc->bsgp', uf, bb_re)
    bu_im = jnp.einsum('bsgc,gpc->bsgp', uf, bb_im)
    a_re = jnp.broadcast_to(ab_re, (1, s) + ab_re.shape)
    a_im = jnp.broadcast_to(ab_im, (1, s) + ab_im.shape)

    def combine(e1, e2):
        a1r, a1i, b1r, b1i = e1
        a2r, a2i, b2r, b2i = e2
        return (a2r * a1r - a2i * a1i,
                a2r * a1i + a2i * a1r,
                a2r * b1r - a2i * b1i + b2r,
                a2r * b1i + a2i * b1r + b2i)

    _, _, x_re, x_im = lax.associative_scan(combine, (a_re, a_im, bu_re, bu_im), axis=1)
    y = (jnp.einsum('bsgp,gcp->bsgc', x_re, c_re.astype(f32))
         - jnp.einsum('bsgp,gcp->bsgc', x_im, c_im.astype(f32)))
    y = y.reshape(bsz, s, SSM_WIDTH) + d_skip.astype(f32) * u.astype(f32)
    g = jax.nn.gelu(y)
    out = g * jax.nn.sigmoid(g @ w_glu.astype(f32) + b_glu.astype(f32))
    return out.astype(u.dtype)

def clamped_swiglu(gu):
    gate = jnp.minimum(gu[:, :D_FF], SWIGLU_LIMIT)
    up = jnp.clip(gu[:, D_FF:], -SWIGLU_LIMIT, SWIGLU_LIMIT)
    return gate * jax.nn.sigmoid(SWIGLU_ALPHA * gate) * (up + 1.0)

def moe_ffn(h, w_router, b_router, w_gu, b_gu, w_dn, b_dn):
    t, d = h.shape
    logits = (h @ w_router + b_router).astype(jnp.float32)
    top_val, top_idx = lax.top_k(logits, TOP_K)
    gates = jax.nn.softmax(top_val, axis=-1)
    n_assign = t * TOP_K
    flat_e = top_idx.reshape(-1)
    flat_tok = jnp.broadcast_to(jnp.arange(t, dtype=jnp.int32)[:, None], (t, TOP_K)).reshape(-1)
    flat_g = gates.reshape(-1)
    order = jnp.argsort(flat_e)
    se = flat_e[order]
    stok = flat_tok[order]
    sg = flat_g[order]
    counts = jnp.bincount(flat_e, length=N_EXPERTS)
    starts = jnp.cumsum(counts) - counts
    padded = (counts + MOE_BLOCK - 1) // MOE_BLOCK * MOE_BLOCK
    pad_end = jnp.cumsum(padded)
    pad_start = pad_end - padded
    dest = pad_start[se] + jnp.arange(n_assign) - starts[se]
    cap = n_assign + N_EXPERTS * MOE_BLOCK
    n_blocks = cap // MOE_BLOCK
    row_tok = jnp.full((cap,), t, dtype=jnp.int32).at[dest].set(stok)
    row_gate = jnp.zeros((cap,), jnp.float32).at[dest].set(sg)
    blk_expert = jnp.minimum(
        jnp.searchsorted(pad_end, jnp.arange(n_blocks) * MOE_BLOCK, side='right'),
        N_EXPERTS - 1)
    h_pad = jnp.concatenate([h, jnp.zeros((1, d), h.dtype)], axis=0)

    def expert_block(args):
        e, toks = args
        xb = h_pad[toks]
        act = clamped_swiglu(xb @ w_gu[e] + b_gu[e])
        return act @ w_dn[e] + b_dn[e]

    y = lax.map(expert_block, (blk_expert, row_tok.reshape(n_blocks, MOE_BLOCK)))
    y = y.reshape(cap, d) * row_gate[:, None].astype(y.dtype)
    return jnp.zeros((t + 1, d), y.dtype).at[row_tok].add(y)[:t]

def setup_inputs(seed: int = 0) -> dict:
    key = jax.random.key(seed)
    ks = jax.random.split(key, 32)
    f32 = jnp.float32
    nrm = lambda k, shape, scale: jax.random.normal(k, shape, f32) * scale
    G, P, C = N_SSM_GROUPS, SSM_STATE, SSM_GROUP
    x = nrm(ks[0], (BATCH, SEQ, D_MODEL), 1.0)
    p = nrm(ks[1], (DEPTH, BATCH, SEQ, PLE_DIM), 1.0)
    norm_mix_g = 1.0 + nrm(ks[2], (DEPTH, D_MODEL), 0.02)
    w_in = nrm(ks[3], (DEPTH, D_MODEL, IN_WIDTH), D_MODEL ** -0.5)
    b_f = jnp.linspace(1.0, 6.0, N_HEADS, dtype=f32)[None, :] + nrm(ks[4], (DEPTH, N_HEADS), 0.1)
    lam_re = -0.5 + nrm(ks[5], (DEPTH, G, P), 0.01)
    lam_im = jnp.broadcast_to(math.pi * jnp.arange(P, dtype=f32), (DEPTH, G, P)) + nrm(ks[6], (DEPTH, G, P), 0.01)
    log_dt = jax.random.uniform(ks[7], (DEPTH, G), f32, math.log(DT_MIN), math.log(DT_MAX))
    b_re = nrm(ks[8], (DEPTH, G, P, C), (2 * C) ** -0.5)
    b_im = nrm(ks[9], (DEPTH, G, P, C), (2 * C) ** -0.5)
    c_re = nrm(ks[10], (DEPTH, G, C, P), (2 * P) ** -0.5)
    c_im = nrm(ks[11], (DEPTH, G, C, P), (2 * P) ** -0.5)
    d_skip = nrm(ks[12], (DEPTH, SSM_WIDTH), 1.0)
    w_glu = nrm(ks[13], (DEPTH, SSM_WIDTH, SSM_WIDTH), SSM_WIDTH ** -0.5)
    b_glu = nrm(ks[14], (DEPTH, SSM_WIDTH), 0.01)
    attn_out_g = 1.0 + nrm(ks[15], (DEPTH, ATTN_WIDTH), 0.02)
    ssm_out_g = 1.0 + nrm(ks[16], (DEPTH, SSM_WIDTH), 0.02)
    w_out = nrm(ks[17], (DEPTH, MIX_WIDTH, D_MODEL), MIX_WIDTH ** -0.5)
    norm_ffn_g = 1.0 + nrm(ks[18], (DEPTH, D_MODEL), 0.02)
    w_router = nrm(ks[19], (DEPTH, D_MODEL, N_EXPERTS), D_MODEL ** -0.5)
    b_router = nrm(ks[20], (DEPTH, N_EXPERTS), 0.01)
    w_gu = nrm(ks[21], (DEPTH, N_EXPERTS, D_MODEL, 2 * D_FF), D_MODEL ** -0.5)
    b_gu = nrm(ks[22], (DEPTH, N_EXPERTS, 2 * D_FF), 0.01)
    w_dn = nrm(ks[23], (DEPTH, N_EXPERTS, D_FF, D_MODEL), D_FF ** -0.5)
    b_dn = nrm(ks[24], (DEPTH, N_EXPERTS, D_MODEL), 0.01)
    norm_ple_g = 1.0 + nrm(ks[25], (DEPTH, D_MODEL), 0.02)
    w_ple_gate = nrm(ks[26], (DEPTH, D_MODEL, D_MODEL), D_MODEL ** -0.5)
    w_ple_proj = nrm(ks[27], (DEPTH, PLE_DIM, D_MODEL), PLE_DIM ** -0.5)
    norm_final_g = 1.0 + nrm(ks[28], (D_MODEL,), 0.02)
    return {"x": x, "p": p, "norm_mix_g": norm_mix_g, "w_in": w_in, "b_f": b_f,
            "lam_re": lam_re, "lam_im": lam_im, "log_dt": log_dt,
            "b_re": b_re, "b_im": b_im, "c_re": c_re, "c_im": c_im,
            "d_skip": d_skip, "w_glu": w_glu, "b_glu": b_glu,
            "attn_out_g": attn_out_g, "ssm_out_g": ssm_out_g, "w_out": w_out,
            "norm_ffn_g": norm_ffn_g, "w_router": w_router, "b_router": b_router,
            "w_gu": w_gu, "b_gu": b_gu, "w_dn": w_dn, "b_dn": b_dn,
            "norm_ple_g": norm_ple_g, "w_ple_gate": w_ple_gate, "w_ple_proj": w_ple_proj,
            "norm_final_g": norm_final_g}

def reference(x, p, norm_mix_g, w_in, b_f, lam_re, lam_im, log_dt, b_re, b_im, c_re, c_im,
              d_skip, w_glu, b_glu, attn_out_g, ssm_out_g, w_out, norm_ffn_g,
              w_router, b_router, w_gu, b_gu, w_dn, b_dn,
              norm_ple_g, w_ple_gate, w_ple_proj, norm_final_g):
    bsz, s, d = x.shape
    split_at = [ATTN_WIDTH, 2 * ATTN_WIDTH, 3 * ATTN_WIDTH, 3 * ATTN_WIDTH + N_HEADS]
    for i in range(DEPTH):
        h = rmsnorm(x, norm_mix_g[i])
        proj = h @ w_in[i]
        q, k, v, f_logit, u = jnp.split(proj, split_at, axis=-1)
        q = q.reshape(bsz, s, N_HEADS, HEAD_DIM)
        k = k.reshape(bsz, s, N_HEADS, HEAD_DIM)
        v = v.reshape(bsz, s, N_HEADS, HEAD_DIM)
        log_f = jax.nn.log_sigmoid(f_logit.astype(jnp.float32) + b_f[i].astype(jnp.float32))
        attn = forgetting_attention(q, k, v, log_f).reshape(bsz, s, ATTN_WIDTH)
        ssm = s5_mixer(u, lam_re[i], lam_im[i], log_dt[i], b_re[i], b_im[i], c_re[i], c_im[i],
                       d_skip[i], w_glu[i], b_glu[i])
        mixed = jnp.concatenate([rmsnorm(attn, attn_out_g[i]), rmsnorm(ssm, ssm_out_g[i])], axis=-1)
        x = x + mixed @ w_out[i]
        h = rmsnorm(x, norm_ffn_g[i]).reshape(bsz * s, d)
        x = x + moe_ffn(h, w_router[i], b_router[i], w_gu[i], b_gu[i], w_dn[i], b_dn[i]).reshape(bsz, s, d)
        gate = jax.nn.sigmoid(rmsnorm(x, norm_ple_g[i]) @ w_ple_gate[i])
        x = x + gate * (p[i] @ w_ple_proj[i])
    return rmsnorm(x, norm_final_g)


_drawn_inputs = setup_inputs


def setup_inputs(seed=0):
    import zlib

    import numpy as np

    out = dict(_drawn_inputs(seed))
    spreads = {}
    factors = {'lam_re': 64.0,
     'b_glu': 6.499,
     'b_gu': 8.0,
     'b_dn': 8.0,
     'norm_ple_g': 50.784,
     'norm_final_g': 7.464,
     'b_re': 2.867,
     'c_im': 2.769}
    for name, (base, spread) in spreads.items():
        noise = np.random.default_rng([zlib.crc32(name.encode()), seed]).standard_normal(out[name].shape)
        drawn = base * np.exp(spread * noise) if base else spread * noise
        out[name] = __import__('jax').numpy.asarray(drawn.astype(out[name].dtype))
    for name, factor in factors.items():
        out[name] = (out[name] * factor).astype(out[name].dtype)
    return out
```

```python
from contextlib import ExitStack
import math

import numpy as np
import concourse.bass as bass
from concourse import mybir

ALU = mybir.AluOpType
ACT = mybir.ActivationFunctionType
F32 = mybir.dt.float32
BF16 = mybir.dt.bfloat16
I32 = mybir.dt.int32
U32 = mybir.dt.uint32
AX_X = mybir.AxisListType.X

P = 128
D = 1024
T = 1024
KT = D // P
HEADS, DH = 8, 64
QT = T // P
CH = 8
NCH = T // CH
SSW = 512
SC = 16
NG = SSW // SC
GP = NG // 2
NB = 4
GB = GP // NB
E = 32
TOPK = 4
W = 256
FT = 8
MAXPASS = E + T * TOPK // W
ROWS = T * TOPK
EPS = 1e-5
WIDTHS = tuple(range(P, W + 1, 8))
FAR = 1e30

O_GMIX, O_GSSM, O_BGLU = 0, 8, 12
O_LR, O_LI, O_LDT = 16, 32, 48
O_BR, O_BI, O_CR, O_CI = 64, 320, 576, 832
N_SMALL = 1088
O_ID, O_TRI, O_IOTA, O_PIDX, O_TID, O_MA = 0, 128, 256, 384, 385, 393
N_CONST = 521

PROJ = ([("u", t) for t in range(8)] + [("v", t) for t in range(8)] + [("f", n) for n in range(2)]
        + [("k", m, n) for m in range(4) for n in range(2)] + [("q", m, n) for m in range(4) for n in range(2)])
PIECES = [(k, b) for b in range(NB) for k in ("prep", "state", "out")]
PIECE_AFTER = {}
_n = 0
for _i, _u in enumerate(PROJ):
    if _u[0] in "vkq":
        _n += 1
        if _n % 2 == 0:
            PIECE_AFTER[_i] = PIECES[_n // 2 - 1]


TILES = [(h, i) for h in range(HEADS) for i in (0, 7, 1, 6, 2, 5, 3, 4)]
LONG = [sum(i >= 4 for _, i in TILES[:s + 1]) for s in range(len(TILES))]


def build(nc, x_cm, x_tm, pT, small, consts, b_f, d_skipT, b_router, gains, w_in, w_glu, w_out,
          w_router, w_gu, w_dn, b_exp, w_ple_gate, w_ple_proj, out, hs, ys):
    with ExitStack() as ctx:
        sem = {}

        def S(name):
            if name not in sem:
                sem[name] = ctx.enter_context(nc.semaphore(name))
            return sem[name]

        base = (nc.sbuf_base + 127) // 128 * 128
        R_Q = base
        R_H = R_Q + 32768
        R_K = R_H + 32768
        R_V = R_K + 32768
        R_PT = R_V + 16640
        R_U = R_PT + 18432
        R_S = R_U + 16384
        R_C = R_S + 48640
        cursor = [R_C]

        def at(name, shape, dt, offset):
            return nc.alloc_sbuf_tensor_at(name, shape, dt, offset=offset)

        def sb(name, shape, dt=F32):
            size = int(np.prod(shape[1:])) * (2 if dt == BF16 else 4)
            t = at(name, shape, dt, cursor[0])
            cursor[0] += (size + 31) // 32 * 32
            return t

        ps = ctx.enter_context(nc.psum_tensor("ps", [P, 8, 512], F32))

        cst = sb("cst", [P, O_MA])
        par = sb("par", [P, N_SMALL])
        ident = cst[:, O_ID:O_ID + P]
        tri = cst[:, O_TRI:O_TRI + P]
        iota32 = cst[:, O_IOTA:O_IOTA + 32]
        iota = cst[:, O_IOTA:O_IOTA + P]
        pidx = cst[:, O_PIDX:O_PIDX + 1]
        tid = cst[:, O_TID:O_TID + 8]
        ones = sb("ones", [P, P])
        ident_b = sb("ident_b", [P, P], BF16)
        mask_qk = sb("mask_qk", [P, P], BF16)
        bf = sb("bf", [8, 1])
        dsk = sb("dsk", [SC, NG])
        brt = sb("brt", [P, 32])
        wf = sb("wf", [P, KT, 8])
        ssum = sb("ssum", [P, 8])
        rstd = sb("rstd", [P, 8])
        asq = sb("asq", [P, QT, HEADS])
        rtok = sb("rtok", [P, 16])
        rden = sb("rden", [P, 2])
        low = sb("low", [P, 4])
        gates = sb("gates", [P, 8, TOPK])
        slots = sb("slots", [P, 8 * TOPK], U32)
        rowid = sb("rowid", [P, 2 * MAXPASS + 4], U32)
        rowc = sb("rowc", [P, 2], U32)
        passtab = sb("passtab", [P, 4], I32)
        passrow = sb("passrow", [1, (MAXPASS + 2) * 4], I32)
        cf = sb("cf", [P, 15, GP])
        pw_r = sb("pw_r", [P, GP, CH + 1])
        pw_i = sb("pw_i", [P, GP, CH + 1])
        pv_r = sb("pv_r", [P, GP, CH])
        pv_i = sb("pv_i", [P, GP, CH])
        sq_r = sb("sq_r", [P, GP, 7])
        sq_i = sb("sq_i", [P, GP, 7])
        assert cursor[0] <= nc.sbuf_usable_end, (cursor[0], nc.sbuf_usable_end)

        hT = at("hT", [P, KT, T], F32, R_H)
        sqx = at("sqx", [P, 2, T], F32, R_K)
        sqa = at("sqa", [P, T], F32, R_K + 12288)
        rbc = at("rbc", [P, T], F32, R_K + 8192)
        rbh = at("rbh", [P, 512], F32, R_PT + 16384)
        w_u = at("w_u", [P, KT, 512], F32, R_PT)
        w_v = at("w_v", [P, KT, 512], F32, R_Q)
        w_k = at("w_k", [P, KT, 512], F32, R_Q + 16384)
        w_q = at("w_q", [P, KT, 512], F32, R_PT)
        zf = at("zf", [8, T], F32, R_Q)
        azf = at("azf", [8, T], F32, R_Q + 4096)
        one8 = at("one8", [8, T], F32, R_Q + 8192)
        qA = at("qA", [P, HEADS, T], F32, R_Q)
        kA = at("kA", [P, HEADS, T], F32, R_K)
        vA = at("vA", [P, QT, HEADS, DH + 1], F32, R_V)
        probs = at("probs", [P, 2, T], F32, R_PT)
        probT = at("probT", [P, 2, QT, P], F32, R_PT + 8192)
        attn = at("attn", [P, QT, 512], F32, R_H)
        attnT = at("attnT", [P, 4, T], F32, R_H + 16384)
        u = at("u", [P, NG, CH, SC], F32, R_U)
        o = R_S
        ugT = at("ugT", [P, 2 * GB, NCH], F32, o); o += 4096
        bm_r = at("bm_r", [P, GB, P], F32, o); o += 2048
        bm_i = at("bm_i", [P, GB, P], F32, o); o += 2048
        toep = at("toep", [P, 2 * GB, P], F32, o); o += 4096
        ca_r = at("ca_r", [P, GB, CH + 1, SC], F32, o); o += 2304
        ca_i = at("ca_i", [P, GB, CH + 1, SC], F32, o); o += 2304
        ba_r = at("ba_r", [P, GB, CH, SC], F32, o); o += 2048
        ba_i = at("ba_i", [P, GB, CH, SC], F32, o); o += 2048
        phi_r = at("phi_r", [P, GB, NCH], F32, o); o += 2048
        phi_i = at("phi_i", [P, GB, NCH], F32, o); o += 2048
        mask_f = at("mask_f", [P, P], F32, o)
        v_r = at("v_r", [P, GB, NCH], F32, o); o += 2048
        v_i = at("v_i", [P, GB, NCH], F32, o); o += 2048
        xs_r = at("xs_r", [P, GB, NCH], F32, o); o += 2048
        xs_i = at("xs_i", [P, GB, NCH], F32, o); o += 2048
        t1 = at("t1", [P, 576], F32, o); o += 2304
        t2 = at("t2", [P, 576], F32, o); o += 2304
        r8t = at("r8t", [P, GB, NCH], F32, o); o += 2048
        ksb = at("ksb", [SC, 2 * GB, P], F32, o); o += 4096
        p1 = at("p1", [P, 576], F32, o); o += 2304
        p2 = at("p2", [P, 576], F32, o); o += 2304
        assert o <= R_C
        wglu = at("wglu", [P, 4, 512], F32, R_S)
        gel = at("gel", [P, NG, CH, SC], F32, R_S + 8192)
        gtm = at("gtm", [P, CH, NG, SC], F32, R_S + 24576)
        gT = at("gT", [P, 4, T], F32, R_K)
        ssmT = at("ssmT", [P, 4, T], F32, R_K + 16384)
        sqs = at("sqs", [P, 4, T], F32, R_S + 8192)
        sgl = at("sgl", [P, 2, 512], F32, R_S + 24576)
        osg = at("osg", [P, 2, 512], F32, R_S + 28672)
        gffn = at("gffn", [P, D], F32, R_S + 40960)
        gatt = at("gatt", [P, 512], F32, R_S + 45312)
        rss = at("rss", [P, 8], F32, R_S + 40960 + 4096)
        wout = at("wout", [P, KT, D], F32, R_V)
        x1 = at("x1", [P, 8, D], F32, R_Q)
        hn = at("hn", [P, 8, D], F32, R_S + 8192)
        h2T = at("h2T", [P, 2, KT, P], F32, R_K)
        wr = at("wr", [P, KT, 32], F32, R_U)
        o = R_U + 1024
        lg = at("lg", [P, 8, 32], F32, o); o += 1024
        m8 = at("m8", [P, 8, 8], F32, o); o += 256
        i8 = at("i8", [P, 8, 8], U32, o); o += 256
        idxf = at("idxf", [P, 8 * TOPK], F32, o); o += 128
        ex4 = at("ex4", [P, 8, TOPK], F32, o); o += 128
        sm4 = at("sm4", [P, 8], F32, o); o += 32
        oh = at("oh", [P, 8, TOPK, 32], F32, o); o += 4096
        sel = at("sel", [P, 8, 32], F32, o); o += 1024
        prf = at("prf", [P, 8, 32], F32, o); o += 1024
        smap = at("smap", [P, 8, 32], F32, o); o += 1024
        rt = at("rt", [P, 12, 32], F32, o); o += 1536
        slf = at("slf", [P, 32], F32, o); o += 128
        tabf = at("tabf", [P, 4], F32, o); o += 32
        psf = at("psf", [P, 32], F32, o); o += 128
        psi = at("psi", [P, 3, 32], I32, o); o += 384
        pcr = at("pcr", [P, 2, 32], F32, o); o += 256
        assert o <= R_S
        o = R_V
        ohc = at("ohc", [P, 32, 2 * MAXPASS + 4], F32, o); o += 128 * (2 * MAXPASS + 4)
        ohr = at("ohr", [P, 32, P], F32, o); o += 16384
        ohp = at("ohp", [P, 8, TOPK, 32], F32, o); o += 4096
        smp = at("smp", [P, 8, 32], F32, o); o += 1024
        assert o <= R_U
        wg = at("wg", [P, FT, KT, 2, P], F32, R_H)
        wd = at("wd", [P, KT, FT, P], F32, R_H + 65536)
        o = R_U
        actT = at("actT", [P, FT, W], F32, o); o += 8192
        gb = at("gb", [P, 2, W], F32, o); o += 2048
        ub = at("ub", [P, 2, W], F32, o); o += 2048
        sg = at("sg", [P, 2, W], F32, o); o += 2048
        tb = at("tb", [P, 2, W], F32, o); o += 2048
        xg = at("xg", [P, 2, D], F32, o); o += 8192
        xT = at("xT", [P, KT, W], F32, o); o += 8192
        yb = at("yb", [P, 2, D], F32, o); o += 8192
        yT = at("yT", [P, 2, W], F32, o); o += 2048
        bin_ = at("bin_", [P, 24], F32, o); o += 96
        bcur = at("bcur", [P, 32], F32, o); o += 128
        assert o <= R_C
        wpg = at("wpg", [P, KT, D], F32, R_H)
        wpp = at("wpp", [P, 2, D], F32, R_H + 32768)
        ppT = at("ppT", [P, 2, 8, P], F32, R_H + 40960)
        grow = at("grow", [P, 2, D], F32, R_H + 49152)
        xn = at("xn", [P, 2, D], F32, R_H + 57344)
        ple_in = at("ple_in", [P, 8, D], F32, R_H + 65536)
        o = R_U
        yg = at("yg", [P, 2, TOPK, D], F32, o); o += 32768
        xnT = at("xnT", [P, 2, KT, P], F32, o); o += 8192
        ot = at("ot", [P, 2, D], F32, o); o += 8192
        sgp = at("sgp", [P, D], F32, o); o += 4096
        sqj = at("sqj", [P, D], F32, o); o += 4096
        assert o <= R_C

        def v_at(h):
            return min(h * (DH + 1), HEADS * (DH + 1) - P)

        block = ctx.enter_context(nc.Block())

        @block.sync
        def _(sp):
            for k in range(KT):
                sp.dma_start(hT[:, k, :], x_cm[:, k, :]).then_inc(S(f"in_ld{k}"), 16)
                if k == 0:
                    sp.dma_start(par[:, :], small).then_inc(S("par_ld"), 16)
                    sp.dma_start(w_u[:, 0:4, :], w_in[:, 0:4, 1544:2056]).then_inc(S("wu_ld"), 16)
                if k == 3:
                    sp.dma_start(w_u[:, 4:8, :], w_in[:, 4:8, 1544:2056]).then_inc(S("wu2_ld"), 16)
            sp.dma_start(w_v[:, :, :], w_in[:, :, 1024:1536]).then_inc(S("wv_ld"), 16)
            sp.dma_start(wf[:, :, :], w_in[:, :, 1536:1544]).then_inc(S("wf_ld"), 16)
            sp.dma_start(w_k[:, :, :], w_in[:, :, 512:1024]).then_inc(S("wk_ld"), 16)
            sp.wait_ge(S("pj_mm"), 8)
            sp.dma_start(w_q[:, :, :], w_in[:, :, 0:512]).then_inc(S("wq_ld"), 16)

            def toeplitz(b):
                sp.wait_ge(S("kd_ready"), b + 1)
                for t in range(CH):
                    sp.dma_start(toep[SC * t:SC * t + SC, :, SC * t:P], ksb[:, :, 0:P - SC * t]).then_inc(S("tp_ld"), 16)

            toeplitz(0)
            toeplitz(1)
            sp.wait_ge(S("cum_ready"), 1)
            sp.wait_ge(S("aug_k"), 1)
            sp.dma_start(kA[65:66, :, :], zf[:, :]).then_inc(S("c_ld"), 16)
            toeplitz(2)
            sp.wait_ge(S("aug_q"), 1)
            sp.dma_start(qA[64:65, :, :], azf[:, :]).then_inc(S("cq_ld"), 16)
            toeplitz(3)
            sp.wait_ge(S("sy_mm"), NB)
            sp.dma_start(wglu[:, :, :], w_glu).then_inc(S("glu_ld"), 16)
            sp.dma_start(gffn[:, :], gains[:, 0:D]).then_inc(S("glu_ld"), 16)
            sp.dma_start(gatt[:, :], gains[:, 3 * D:3 * D + 512]).then_inc(S("glu_ld"), 16)
            sp.wait_ge(S("s_mm"), len(TILES))
            sp.dma_start(x1[:, :, :], x_tm).then_inc(S("out_ld"), 16)
            sp.wait_ge(S("pv_mm"), len(TILES))
            sp.dma_start(wout[:, :, :], w_out).then_inc(S("out_ld"), 16)
            sp.wait_ge(S("gt_mm"), 8)
            sp.dma_start(wr[:, :, :], w_router).then_inc(S("out_ld"), 16)
            for t in range(8):
                sp.wait_ge(S("hn_ready"), t + 1)
                sp.dma_start(hs[t * P:t * P + P, :], hn[:, t, :]).then_inc(S("hs_st"), 16)
            sp.wait_ge(S("tab_ready"), 1)
            sp.dma_start(passrow[0:1, :], passtab[0:MAXPASS + 2, :]).then_inc(S("tab_ld"), 16)
            sp.wait_ge(S("tab_ld"), 16)
            npass = sp.value_load(passrow[0:1, 3:4], min_val=T * TOPK // W, max_val=MAXPASS)

            def wait_at(name, value):
                sp.wait_ge(S(name), value)
                sp.sem_inc(S("sp_passed"), 1)

            def table(b):
                e = sp.value_load(passrow[0:1, bass.ds(4 * b, 1)], min_val=0, max_val=E - 1)
                return e

            def gu_chunk(e, f):
                sp.dma_start(wg[:, f], w_gu[bass.ds(e, 1), f].rearrange("o p k g m -> (o p) k g m")).then_inc(S(f"in_ld{f}"), 16)

            def dn_chunk(e, j):
                sp.dma_start(wd[:, 2 * j:2 * j + 2], w_dn[bass.ds(e, 1), j].rearrange("o p d k m -> (o p) d k m")
                             ).then_inc(S(f"dn_ld{j}"), 16)

            sp.wait_ge(S("rt_mm"), 8)
            sp.wait_ge(S("rt_evac"), 8)
            e0 = table(0)
            sp.wait_ge(S("id_mm"), 1)
            for f in range(FT):
                gu_chunk(e0, f)
            for j in range(KT // 2):
                dn_chunk(e0, j)
            with sp.Fori(1, npass) as b:
                e = table(b)
                for f in range(FT):
                    wait_at("gu_mm", b * FT - FT + f + 1)
                    gu_chunk(e, f)
                for j in range(KT // 2):
                    wait_at("dn_mm", b * KT - KT + 2 * j + 2)
                    dn_chunk(e, j)
            wait_at("gu_mm", npass * FT)
            sp.dma_start(wpp[:, :, :], w_ple_proj).then_inc(S("wpp_ld"), 16)
            sp.dma_start(ppT[:, :, :, :], pT).then_inc(S("wpp_ld"), 16)
            sp.dma_start(grow[:, :, :], gains[:, D:3 * D].rearrange("p (a d) -> p a d", a=2)).then_inc(S("wp_ld"), 16)
            sp.dma_start(wpg[:, :, :], w_ple_gate).then_inc(S("wp_ld"), 16)
            for t in range(8):
                sp.wait_ge(S("o_ready"), t + 1)
                sp.dma_start(out[:, t, :], ot[:, t % 2, :]).then_inc(S(f"o_st{t % 2}"), 16)
            sp.wait_ge(S("o_st0"), 64)
            sp.wait_ge(S("o_st1"), 64)

        @block.gpsimd
        def _(pool):
            g = nc.gpsimd
            chain = [0]

            def link(ins):
                chain[0] += 1
                ins.then_inc(S("pool_chain"), 1)
                pool.wait_ge(S("pool_chain"), chain[0])

            pool.dma_start(cst[:, :], consts[:, 0:O_MA]).then_inc(S("small_ld"), 16)
            pool.dma_start(mask_f[:, :], consts[:, O_MA:N_CONST]).then_inc(S("small_ld"), 16)
            pool.dma_start(bf[:, :], b_f).then_inc(S("small_ld"), 16)
            pool.dma_start(dsk[:, :], d_skipT).then_inc(S("small_ld"), 16)
            pool.dma_start(brt[:, :], b_router).then_inc(S("small_ld"), 16)
            link(g.memset(toep[:, :, :], 0.0))
            pool.wait_ge(S("par_ld"), 16)
            pool.wait_ge(S("small_ld"), 80)

            cr = par[:, O_CR:O_CR + GP * SC].rearrange("p (g c) -> p g c", c=SC)
            ci = par[:, O_CI:O_CI + GP * SC].rearrange("p (g c) -> p g c", c=SC)
            bbr = par[:, O_BR:O_BR + GP * SC].rearrange("p (g c) -> p g c", c=SC)
            bbi = par[:, O_BI:O_BI + GP * SC].rearrange("p (g c) -> p g c", c=SC)
            p1c = p1[:, :].rearrange("p (g t c) -> p g t c", g=GB, c=SC)
            p2c = p2[:, :].rearrange("p (g t c) -> p g t c", g=GB, c=SC)
            p1b = p1[:, 0:512].rearrange("p (g t c) -> p g t c", g=GB, c=SC)
            p2b = p2[:, 0:512].rearrange("p (g t c) -> p g t c", g=GB, c=SC)
            p1j = p1[:, 0:512].rearrange("p (g j) -> p g j", g=GB)
            p2j = p2[:, 0:512].rearrange("p (g j) -> p g j", g=GB)

            def bc(a, n):
                return a.unsqueeze(2).to_broadcast([P, GB, n, SC])

            def bt(a, n):
                return a.unsqueeze(3).to_broadcast([P, GB, n, SC])

            pool.wait_ge(S("coef_ready"), 1)
            for b in range(NB):
                gs = slice(GB * b, GB * b + GB)
                if b:
                    pool.wait_ge(S("sy_mm"), b)
                g.tensor_tensor(p1c, bc(cr[:, gs], CH + 1), bt(pw_i[:, gs], CH + 1), ALU.mult)
                link(g.tensor_tensor(p2c, bc(ci[:, gs], CH + 1), bt(pw_r[:, gs], CH + 1), ALU.mult))
                link(g.tensor_tensor(p1c, p1c, p2c, ALU.add))
                link(g.tensor_scalar(ca_i[:, :, :, :], p1c, -1.0, 1.0, ALU.mult, ALU.mult))
                g.tensor_tensor(p1b, bt(pv_r[:, gs], CH), bc(bbi[:, gs], CH), ALU.mult)
                link(g.tensor_tensor(p2b, bt(pv_i[:, gs], CH), bc(bbr[:, gs], CH), ALU.mult))
                g.tensor_tensor(ba_i[:, :, :, :], p1b, p2b, ALU.add).then_inc(S("coef_i"), 1)
                pool.wait_ge(S("coef_i"), b + 1)
                g.memset(phi_r[:, :, 0:1], 1.0)
                link(g.memset(phi_i[:, :, 0:1], 0.0))
                for k in range(7):
                    n = 1 << k
                    sr = sq_r[:, gs, k:k + 1].to_broadcast([P, GB, n])
                    si = sq_i[:, gs, k:k + 1].to_broadcast([P, GB, n])
                    q1 = p1[:, 0:GB * n].rearrange("p (g j) -> p g j", g=GB)
                    q2 = p2[:, 0:GB * n].rearrange("p (g j) -> p g j", g=GB)
                    g.tensor_tensor(q1, phi_r[:, :, 0:n], sr, ALU.mult)
                    link(g.tensor_tensor(q2, phi_i[:, :, 0:n], si, ALU.mult))
                    link(g.tensor_tensor(phi_r[:, :, n:2 * n], q1, q2, ALU.subtract))
                    g.tensor_tensor(q1, phi_r[:, :, 0:n], si, ALU.mult)
                    link(g.tensor_tensor(q2, phi_i[:, :, 0:n], sr, ALU.mult))
                    ins = g.tensor_tensor(phi_i[:, :, n:2 * n], q1, q2, ALU.add)
                    link(ins)
                g.memset(xs_i[:, :, 0:1], 0.0).then_inc(S("phi_ready"), 1)
                for s in range(2 * GB):
                    ch = 2 * GB * b + s
                    g.tensor_scalar(p1[0:SC, SC * s:SC * s + SC], cst[0:SC, O_ID:O_ID + SC], dsk[:, ch:ch + 1], 1.0,
                                    ALU.mult, ALU.mult)
                pool.wait_ge(S("k_evac"), b + 1)
                link(g.memset(p2[0:SC, 0:1], 0.0))
                g.tensor_tensor(ksb[:, :, 0:SC], ksb[:, :, 0:SC],
                                p1[0:SC, 0:2 * GB * SC].rearrange("p (s c) -> p s c", c=SC), ALU.add).then_inc(S("kd_ready"), 1)
                pool.wait_ge(S("kd_ready"), b + 1)
                pool.wait_ge(S("scan_done"), b + 1)
                w_r = t1[:, 0:512].rearrange("p (g j) -> p g j", g=GB)
                w_i = t2[:, 0:512].rearrange("p (g j) -> p g j", g=GB)
                g.tensor_tensor(p1j, phi_i[:, :, :], w_r, ALU.mult)
                link(g.tensor_tensor(p2j, phi_r[:, :, :], w_i, ALU.mult))
                g.tensor_tensor(xs_i[:, :, 1:NCH], p1j[:, :, 0:NCH - 1], p2j[:, :, 0:NCH - 1], ALU.add).then_inc(S("xi_ready"), 1)
                pool.wait_ge(S("xi_ready"), b + 1)
            pool.wait_ge(S("sy_evac"), NB)
            link(g.tensor_tensor(gel[:, :, :, :].rearrange("p g t c -> p (g t c)"), u[:, :, :, :].rearrange("p g t c -> p (g t c)"), u[:, :, :, :].rearrange("p g t c -> p (g t c)"), ALU.mult))
            link(g.tensor_scalar(gel[:, :, :, :].rearrange("p g t c -> p (g t c)"), gel[:, :, :, :].rearrange("p g t c -> p (g t c)"), 0.044715, 1.0, ALU.mult, ALU.add))
            g.tensor_tensor(gel[:, :, :, :].rearrange("p g t c -> p (g t c)"), gel[:, :, :, :].rearrange("p g t c -> p (g t c)"), u[:, :, :, :].rearrange("p g t c -> p (g t c)"), ALU.mult).then_inc(S("gel_in"), 1)
            pool.wait_ge(S("gel_th"), 1)
            link(g.tensor_scalar(gel[:, :, :, :].rearrange("p g t c -> p (g t c)"), gel[:, :, :, :].rearrange("p g t c -> p (g t c)"), 1.0, 0.5, ALU.add, ALU.mult))
            g.tensor_tensor(gtm[:, :, :, :].rearrange("p t g c -> p g t c"), gel[:, :, :, :], u[:, :, :, :], ALU.mult).then_inc(S("gel_out"), 1)

            def gather(half):
                g.indirect_dma_start(xg[:, half, :], None, hs[:, :], bass.IndirectOffsetOnAxis(ap=rowc[:, half:half + 1], axis=0)
                                     ).then_inc(S(f"rows{half}_ld"), 16)

            pool.wait_ge(S("rowid_ready"), 1)
            pool.wait_ge(S("hs_st"), 16 * 8)
            g.tensor_copy(rowc[:, :], rowid[:, 0:2]).then_inc(S("rowc_ready"), 1)
            pool.wait_ge(S("rowc_ready"), 1)
            gather(0)
            gather(1)
            pool.wait_ge(S("tab_ld"), 16)
            npass = pool.value_load(passrow[0:1, 3:4], min_val=T * TOPK // W, max_val=MAXPASS)
            e0 = pool.value_load(passrow[0:1, 0:1], min_val=0, max_val=E - 1)
            pool.dma_start(bin_[:, :], b_exp[bass.ds(e0, 1)].rearrange("o p c -> (o p) c")).then_inc(S("be_ld"), 16)
            pool.sem_inc(S("y_free"), 1)

            def wait_at(name, value):
                pool.wait_ge(S(name), value)
                pool.sem_inc(S("pool_passed"), 1)

            def gather_pass(b, ahead):
                n_then = pool.value_load(passrow[0:1, bass.ds(4 * b + 4 * ahead + 2, 1)], min_val=0, max_val=W)
                wait_at("xp_mm", 2 * b + 2 * ahead)
                wait_at("xp2_mm", 2 * b + 2 * ahead)
                g.tensor_copy(rowc[:, :], rowid[:, bass.ds(2 * b + 2 * ahead, 2)]).then_inc(S("rowc_ready"), 1)
                wait_at("rowc_ready", b + ahead + 1)
                gather(0)
                with pool.If(n_then > P):
                    gather(1)
                with pool.Else():
                    pool.dma_start(xg[:, 1, 0:32], b_router).then_inc(S("rows1_ld"), 16)

            gather_pass(0, 1)
            with pool.Fori(0, npass) as b:
                e = pool.value_load(passrow[0:1, bass.ds(4 * b + 4, 1)], min_val=0, max_val=E - 1)
                r0 = pool.value_load(passrow[0:1, bass.ds(4 * b + 1, 1)], min_val=0, max_val=ROWS)
                n = pool.value_load(passrow[0:1, bass.ds(4 * b + 2, 1)], min_val=0, max_val=W)
                wait_at("be_used", b + 1)
                pool.dma_start(bin_[:, :], b_exp[bass.ds(e, 1)].rearrange("o p c -> (o p) c")).then_inc(S("be_ld"), 16)
                gather_pass(b, 2)
                wait_at("y_evac", b * KT + KT + 3)
                with pool.If(n > P):
                    pool.dma_start(ys[bass.ds(r0, W), :].rearrange("(a p) d -> p a d", p=P), yb[:, :, :]).then_inc(S("y_st"), 16)
                with pool.Else():
                    pool.dma_start(ys[bass.ds(r0, P), :], yb[:, 0, :]).then_inc(S("y_st"), 16)
                pool.wait_ge(S("y_st"), b * 16 + 16)
                pool.sem_inc(S("y_free"), 1)
            wait_at("be_ld", npass * 16 + 16)
            wait_at("rows0_ld", npass * 16 + 32)
            wait_at("rows1_ld", npass * 16 + 32)
            pool.wait_ge(S("slots_ready"), 1)
            for t in range(8):
                if t >= 2:
                    pool.wait_ge(S("yg_used"), t - 1)
                for k in range(TOPK):
                    g.indirect_dma_start(yg[:, t % 2, k, :], None, ys[0:ROWS, :],
                                         bass.IndirectOffsetOnAxis(ap=slots[:, t * TOPK + k:t * TOPK + k + 1], axis=0)
                                         ).then_inc(S(f"yg_ld{t % 2}"), 16)

        @block.scalar
        def _(act):
            a = nc.scalar
            for k in range(KT):
                act.wait_ge(S(f"in_ld{k}"), 16)
                if k >= 3:
                    act.wait_ge(S("sq_added"), k - 2)
                a.activation(sqx[:, k % 2, :] if k else sqa[:, :], hT[:, k, :], ACT.Square).then_inc(S("sq_ready"), 1)
            act.wait_ge(S("rtok_mm"), 1)
            a.activation(rtok[:, :], ps[:, 6, 0:16], ACT.Sqrt).then_inc(S("sd_ready"), 1)
            a.activation(rbh[:, :], rbh[:, :], ACT.Sqrt).then_inc(S("sd_ready"), 1)
            def piece(kind, b):
                if kind == "prep":
                    act.wait_ge(S("ut_mm"), b + 1)
                    a.activation(ugT[:, :, :], ps[:, 0:2, :].rearrange("p b (s j) -> p (b s) j", j=NCH), ACT.Copy).then_inc(S("ut_evac"), 1)
                    act.wait_ge(S("bt_mm"), b + 1)
                    a.activation(bm_r[:, :, :], ps[:, 6, :].rearrange("p (s j) -> p s j", j=P), ACT.Copy)
                    a.activation(bm_i[:, :, :], ps[:, 7, :].rearrange("p (s j) -> p s j", j=P), ACT.Copy).then_inc(S("bt_evac"), 1)
                    act.wait_ge(S("kk_mm"), b + 1)
                    a.activation(ksb[:, :, :].rearrange("p (g s) j -> p s g j", s=2), ps[0:SC, 0:2, :].rearrange("p s (g j) -> p s g j", j=NCH), ACT.Copy).then_inc(S("k_evac"), 1)
                if kind == "out":
                    act.wait_ge(S("sy_mm"), b + 1)
                    for s in range(2):
                        g0 = 2 * b * GB
                        ins = a.activation(u[:, g0 + s:g0 + 2 * GB:2].rearrange("p g t c -> p g (t c)"), ps[:, s, :].rearrange("p (g n) -> p g n", g=GB), ACT.Copy)
                    ins.then_inc(S("sy_evac"), 1)

            def s5_angles():
                act.wait_ge(S("par_ld"), 16)
                act.wait_ge(S("small_ld"), 80)
                a.activation(cf[:, 0, :], par[:, O_LDT:O_LDT + GP], ACT.Exp).then_inc(S("dt_ready"), 1)
                act.wait_ge(S("ang_ready"), 1)
                a.activation(cf[:, 2, :], cf[:, 1, :], ACT.Exp)
                a.activation(cf[:, 3, :], cf[:, 1, :], ACT.Exp, scale=float(CH))
                a.activation(cf[:, 6, :], cf[:, 4, :], ACT.Sin)
                a.activation(cf[:, 7, :], cf[:, 5, :], ACT.Sin).then_inc(S("trig_ready"), 1)

            for i, un in enumerate(PROJ):
                bank = 2 + i % 4
                if un[0] in "uv":
                    act.wait_ge(S("pj_mm"), i + 1)
                    act.wait_ge(S("rtok_ready"), 1)
                if un[0] == "u":
                    a.activation(u[:, :, un[1], :], ps[:, bank, :].rearrange("p (g c) -> p g c", c=SC), ACT.Copy,
                                 scale=rtok[:, un[1]:un[1] + 1]).then_inc(S("pj_evac"), 1)
                    if un[1] == 3:
                        s5_angles()
                elif un[0] == "v":
                    a.activation(vA[:, un[1], :, 0:DH], ps[:, bank, :].rearrange("p (h d) -> p h d", d=DH), ACT.Copy,
                                 scale=rtok[:, 8 + un[1]:9 + un[1]]).then_inc(S("pj_evac"), 1)
                elif un[0] == "f":
                    if un[1] == 0:
                        act.wait_ge(S("rtok_mm"), 1)
                        a.activation(kA[64:66, :, :].rearrange("p h t -> p (h t)"), ones[64:66, 0:1].to_broadcast([2, HEADS * T]),
                                     ACT.Copy).then_inc(S("aug_k"), 1)
                    if un[1] == 1:
                        act.wait_ge(S("lf_in"), 1)
                        a.activation(azf[:, :], azf[:, :], ACT.Exp, scale=-1.0).then_inc(S("act_chain"), 1)
                        act.wait_ge(S("act_chain"), 1)
                        a.activation(azf[:, :], azf[:, :], ACT.Ln, bias=1.0).then_inc(S("lf_out"), 1)
                if un == ("k", 3, 1):
                    act.wait_ge(S("c_ld"), 16)
                    act.wait_ge(S("pj_mm"), i + 1)
                    a.activation(qA[64:66, :, :].rearrange("p h t -> p (h t)"), ones[64:66, 0:1].to_broadcast([2, HEADS * T]),
                                 ACT.Copy).then_inc(S("aug_q"), 1)
                if i in PIECE_AFTER:
                    piece(*PIECE_AFTER[i])

            def exp(s):
                _, i = TILES[s]
                act.wait_ge(S("low_ready"), s + 1)
                if s >= 2:
                    act.wait_ge(S("pa_mm"), s - 1)
                    if LONG[s - 2]:
                        act.wait_ge(S("pb_mm"), LONG[s - 2])
                slot = 2 * (s % 2)
                a.activation(probs[:, s % 2, 0:(i + 1) * P], ps[:, slot:slot + 2, :].rearrange("p b n -> p (b n)")[:, 0:(i + 1) * P],
                             ACT.Exp, bias=low[:, s % 4:s % 4 + 1], scale=-1.0).then_inc(S("exp_done"), 1)

            def first_keys(s):
                _, i = TILES[s]
                n = min(i + 1, 4)
                act.wait_ge(S("pa_mm"), s + 1)
                if s >= 2:
                    act.wait_ge(S("pv_mm"), s - 1)
                a.activation(probT[:, s % 2, 0:n, :], ps[:, 4, 0:n * P].rearrange("p (k q) -> p k q", q=P), ACT.Copy).then_inc(S("pa_evac"), 1)

            def squares_out(s):
                h, i = TILES[s]
                act.wait_ge(S("pv_evac"), s + 1)
                a.activation(attnT[:, 0, DH * (s % 8):DH * (s % 8) + DH], attn[:, i, DH * h:DH * h + DH], ACT.Square,
                             accum_out=asq[:, i, h:h + 1]).then_inc(S("as_ready"), 1)

            exp(0)
            exp(1)
            for s in range(len(TILES)):
                first_keys(s)
                if s + 2 < len(TILES):
                    exp(s + 2)
                if s >= 2:
                    squares_out(s - 2)
                if s == len(TILES) // 2:
                    act.wait_ge(S("gel_in"), 1)
                    a.activation(gel[:, :, :, :].rearrange("p g t c -> p (g t c)"), gel[:, :, :, :].rearrange("p g t c -> p (g t c)"), ACT.Tanh, scale=math.sqrt(2 / math.pi)).then_inc(S("gel_th"), 1)

            squares_out(len(TILES) - 2)
            squares_out(len(TILES) - 1)

            for t in range(8):
                act.wait_ge(S("gt_mm"), t + 1)
                a.activation(gT[:, :, t * P:t * P + P], ps[:, t % 4, :].rearrange("p (c j) -> p c j", c=4), ACT.Copy).then_inc(S("gt_evac"), 1)
            act.wait_ge(S("am_ready"), 1)
            a.activation(ssum[:, :], ssum[:, :], ACT.Sqrt).then_inc(S("ad_ready"), 1)
            for n in range(8):
                co, hf = n // 2, n % 2
                act.wait_ge(S("gl_mm"), n + 1)
                a.activation(sgl[:, n % 2, :], ps[:, 4 + n % 2, :], ACT.Sigmoid, bias=par[:, O_BGLU + co:O_BGLU + co + 1]).then_inc(S("gl_sig"), 1)
                act.wait_ge(S("gl_out"), n + 1)
                a.activation(sqs[:, co, hf * 512:hf * 512 + 512], osg[:, n % 2, :], ACT.Square)
                a.activation(ssmT[:, co, hf * 512:hf * 512 + 512], osg[:, n % 2, :], ACT.Copy,
                             scale=par[:, O_GSSM + co:O_GSSM + co + 1]).then_inc(S("ssm_ready"), 1)
            for i in range(QT):
                act.wait_ge(S("at_mm"), i + 1)
                a.activation(attnT[:, :, i * P:i * P + P], ps[:, i % 4, :].rearrange("p (c j) -> p c j", c=4), ACT.Copy).then_inc(S("at_evac"), 1)
            act.wait_ge(S("sm_ready"), 1)
            a.activation(rss[:, :], rss[:, :], ACT.Sqrt).then_inc(S("sd2_ready"), 1)
            def ffn_norm(t):
                act.wait_ge(S("x1_ready"), t + 1)
                a.activation(hn[:, t, :], x1[:, t, :], ACT.Square, accum_out=ssum[:, t:t + 1]).then_inc(S("row_sq"), 1)
                act.wait_ge(S("row_ms"), t + 1)
                a.activation(ssum[:, t:t + 1], ssum[:, t:t + 1], ACT.Sqrt).then_inc(S("row_sd"), 1)

            def router_in(t):
                act.wait_ge(S("ht_mm"), t + 1)
                a.activation(h2T[:, t % 2, :, :].rearrange("p k j -> p (k j)"), ps[:, 4:6, :].rearrange("p b n -> p (b n)"),
                             ACT.Copy).then_inc(S("ht_evac"), 1)

            for t in range(8):
                ffn_norm(t)
                router_in(t)
            act.wait_ge(S("top_ready"), 1)
            a.activation(ex4[:, :, :], ex4[:, :, :], ACT.Exp).then_inc(S("ge_ready"), 1)

            act.wait_ge(S("tab_ld"), 16)
            npass = act.value_load(passrow[0:1, 3:4], min_val=T * TOPK // W, max_val=MAXPASS)

            def xt_half(a_, turned, done, count):
                for j in range(2):
                    act.wait_ge(S(turned), count + j + 1)
                    a.activation(xT[:, 4 * j:4 * j + 4, a_ * P:a_ * P + P], ps[:, 6 - 2 * a_ + j, :].rearrange("p (k q) -> p k q", q=P),
                                 ACT.Copy).then_inc(S(done), 1)

            def xt_rows(n, count):
                xt_half(0, "xp_mm", "xt_evac", count)
                with act.If(n > P):
                    xt_half(1, "xp2_mm", "xt2_evac", count)
                with act.Else():
                    act.wait_ge(S("xp2_mm"), count + 2)
                    act.sem_inc(S("xt2_evac"), 2)

            def y_out(d, count):
                act.wait_ge(S("yt_mm"), count)
                a.activation(yb[:, :, d * P:d * P + P], ps[:, 4 + d % 2, 0:W].rearrange("p (a d) -> p a d", a=2),
                             ACT.Copy).then_inc(S("y_evac"), 1)

            act.wait_ge(S("hs_st"), 16 * 8)
            xt_rows(act.value_load(passrow[0:1, 2:3], min_val=0, max_val=W), 0)
            act.sem_inc(S("y_evac"), 2)
            with act.Fori(0, npass) as b:
                n_next = act.value_load(passrow[0:1, bass.ds(4 * b + 6, 1)], min_val=0, max_val=W)
                for f in range(FT):
                    act.wait_ge(S("g_ready"), b * FT + f + 1)
                    a.activation(sg[:, f % 2, :], gb[:, f % 2, :], ACT.Sigmoid, scale=1.702).then_inc(S("sig_ready"), 1)
                    if f == 0:
                        y_out(KT - 1, b * KT + 2)
                xt_rows(n_next, b * 2 + 2)
                act.wait_ge(S("y_free"), b + 1)
                for d in range(KT - 1):
                    y_out(d, b * KT + d + 3)
            y_out(KT - 1, npass * KT + 2)

            def ple_norm(t):
                act.wait_ge(S("x2_ready"), t + 1)
                a.activation(sqj[:, :], x1[:, t, :], ACT.Square, accum_out=ssum[:, t:t + 1]).then_inc(S("row_sq"), 1)
                act.wait_ge(S("row_ms"), t + 9)
                a.activation(ssum[:, t:t + 1], ssum[:, t:t + 1], ACT.Sqrt).then_inc(S("row_sd"), 1)

            def gate_in(t):
                act.wait_ge(S("nt_mm"), t + 1)
                a.activation(xnT[:, t % 2, :, :].rearrange("p k j -> p (k j)"), ps[:, 0:2, :].rearrange("p b n -> p (b n)"),
                             ACT.Copy).then_inc(S("nt_evac"), 1)

            def ple_gate(t, n):
                act.wait_ge(S("pg_mm"), 2 * t + n + 1)
                if t:
                    act.wait_ge(S("x3_half"), 2 * t + n - 1)
                a.activation(sgp[:, n * 512:n * 512 + 512], ps[:, 2 + n, :], ACT.Sigmoid).then_inc(S("pg_sig"), 1)

            def fin_norm(t):
                act.wait_ge(S("x3_half"), 2 * t + 2)
                a.activation(sqj[:, :], x1[:, t, :], ACT.Square, accum_out=rstd[:, t:t + 1]).then_inc(S("zs_ready"), 1)
                act.wait_ge(S("zm_ready"), t + 1)
                a.activation(rstd[:, t:t + 1], rstd[:, t:t + 1], ACT.Sqrt).then_inc(S("zd_ready"), 1)

            for i in range(16):
                act.wait_ge(S("pp_mm"), i + 1)
                a.activation(ple_in[:, i // 2, 512 * (i % 2):512 * (i % 2) + 512], ps[:, 4 + i % 4, :], ACT.Copy).then_inc(S("pp_evac"), 1)
            ple_norm(0)
            gate_in(0)
            ple_norm(1)
            for t in range(8):
                if t + 2 < 8:
                    ple_norm(t + 2)
                ple_gate(t, 0)
                if t + 1 < 8:
                    gate_in(t + 1)
                ple_gate(t, 1)
                fin_norm(t)

        @block.vector
        def _(dve):
            v = nc.vector
            chain = [0]

            def link(ins):
                chain[0] += 1
                ins.then_inc(S("dve_chain"), 1)
                dve.wait_ge(S("dve_chain"), chain[0])

            v.memset(ones[:, :], 1.0).then_inc(S("ones_ready"), 1)
            link(v.memset(vA[:, :, :, DH:DH + 1], 1.0))
            lr, li = par[:, O_LR:O_LR + GP], par[:, O_LI:O_LI + GP]
            C = lambda i: cf[:, i, :]
            tt = lambda o_, a_, b_, op: link(v.tensor_tensor(o_, a_, b_, op))

            def angles():
                dve.wait_ge(S("dt_ready"), 1)
                tt(C(1), lr, C(0), ALU.mult)
                tt(C(8), li, C(0), ALU.mult)
                two_pi = 2 * math.pi
                c1 = 6.28125
                c2 = float(np.float32(round((two_pi - c1) * 2 ** 20) / 2 ** 20))
                c3 = two_pi - c1 - c2
                magic = 12582912.0
                for dst, turn in ((4, 0.0), (5, 0.25)):
                    link(v.tensor_scalar(C(9), C(8), 1.0 / two_pi, turn, ALU.mult, ALU.add))
                    link(v.tensor_scalar(C(9), C(9), magic, -magic, ALU.add, ALU.add))
                    link(v.scalar_tensor_tensor(C(10), C(9), -c1, C(8), ALU.mult, ALU.add))
                    link(v.scalar_tensor_tensor(C(10), C(9), -c2, C(10), ALU.mult, ALU.add))
                    link(v.scalar_tensor_tensor(C(10), C(9), -c3, C(10), ALU.mult, ALU.add))
                    link(v.tensor_scalar(C(10), C(10), turn * two_pi, 3.1415925, ALU.add, ALU.min))
                    ins = v.tensor_scalar(C(dst), C(10), -3.1415925, None, ALU.max)
                    if dst == 5:
                        ins.then_inc(S("ang_ready"), 1)
                    else:
                        link(ins)

            def cmul(o_r, o_i, a_r, a_i, b_r, b_i, x, y):
                v.tensor_tensor(x, a_r, b_r, ALU.mult)
                link(v.tensor_tensor(y, a_i, b_i, ALU.mult))
                link(v.tensor_tensor(o_r, x, y, ALU.subtract))
                v.tensor_tensor(x, a_r, b_i, ALU.mult)
                link(v.tensor_tensor(y, a_i, b_r, ALU.mult))
                link(v.tensor_tensor(o_i, x, y, ALU.add))

            br_ = par[:, O_BR:O_BR + GP * SC].rearrange("p (g c) -> p g c", c=SC)
            bi_ = par[:, O_BI:O_BI + GP * SC].rearrange("p (g c) -> p g c", c=SC)
            cr_ = par[:, O_CR:O_CR + GP * SC].rearrange("p (g c) -> p g c", c=SC)
            ci_ = par[:, O_CI:O_CI + GP * SC].rearrange("p (g c) -> p g c", c=SC)

            def coefficients():
                dve.wait_ge(S("trig_ready"), 1)
                v.tensor_tensor(pw_r[:, :, 1], C(2), C(7), ALU.mult)
                link(v.tensor_tensor(pw_i[:, :, 1], C(2), C(6), ALU.mult))
                v.memset(pw_r[:, :, 0:1], 1.0)
                v.memset(pw_i[:, :, 0:1], 0.0)
                v.tensor_scalar(C(9), pw_r[:, :, 1], -1.0, None, ALU.add)
                v.tensor_tensor(C(10), lr, lr, ALU.mult)
                link(v.tensor_tensor(C(11), li, li, ALU.mult))
                tt(C(10), C(10), C(11), ALU.add)
                link(v.reciprocal(C(10), C(10)))
                v.tensor_tensor(C(11), C(9), lr, ALU.mult)
                link(v.tensor_tensor(C(12), pw_i[:, :, 1], li, ALU.mult))
                tt(C(11), C(11), C(12), ALU.add)
                v.tensor_tensor(C(13), pw_i[:, :, 1], lr, ALU.mult)
                link(v.tensor_tensor(C(14), C(9), li, ALU.mult))
                tt(C(13), C(13), C(14), ALU.subtract)
                v.tensor_tensor(C(11), C(11), C(10), ALU.mult)
                link(v.tensor_tensor(C(13), C(13), C(10), ALU.mult))
                zr = C(11).unsqueeze(2).to_broadcast([P, GP, SC])
                zi = C(13).unsqueeze(2).to_broadcast([P, GP, SC])
                T1 = t1[:, 0:256].rearrange("p (g c) -> p g c", c=SC)
                T2 = t2[:, 0:256].rearrange("p (g c) -> p g c", c=SC)
                T3 = t1[:, 256:512].rearrange("p (g c) -> p g c", c=SC)
                T4 = t2[:, 256:512].rearrange("p (g c) -> p g c", c=SC)
                v.tensor_tensor(T1, zr, br_, ALU.mult)
                v.tensor_tensor(T2, zi, bi_, ALU.mult)
                v.tensor_tensor(T3, zr, bi_, ALU.mult)
                link(v.tensor_tensor(T4, zi, br_, ALU.mult))
                v.tensor_tensor(br_, T1, T2, ALU.subtract)
                link(v.tensor_tensor(bi_, T3, T4, ALU.add))
                pr, pi = pw_r, pw_i
                x = lambda n: t1[:, 0:GP * n].rearrange("p (g n) -> p g n", n=n)
                y = lambda n: t2[:, 0:GP * n].rearrange("p (g n) -> p g n", n=n)
                for lo, n in ((1, 1), (2, 2), (4, 4)):
                    sr = pr[:, :, lo:lo + 1].to_broadcast([P, GP, n])
                    si = pi[:, :, lo:lo + 1].to_broadcast([P, GP, n])
                    cmul(pr[:, :, lo + 1:lo + 1 + n], pi[:, :, lo + 1:lo + 1 + n], pr[:, :, 1:1 + n], pi[:, :, 1:1 + n], sr, si, x(n), y(n))
                for t in range(CH):
                    v.tensor_copy(pv_r[:, :, t], pr[:, :, CH - 1 - t])
                    ins = v.tensor_copy(pv_i[:, :, t], pi[:, :, CH - 1 - t])
                link(ins)
                src = (C(7), C(6))
                for k in range(9):
                    if k < 2:
                        dst = (C(4 + k * 4), C(5 + k * 4))
                    else:
                        dst = (sq_r[:, :, k - 2], sq_i[:, :, k - 2])
                    cmul(dst[0], dst[1], src[0], src[1], src[0], src[1], C(12), C(14))
                    src = dst
                v.memset(xs_r[:, :, 0:1], 0.0)
                v.memset(r8t[:, :, 0:1], 0.0).then_inc(S("coef_ready"), 1)

            def batch_coef(b):
                gs = slice(GB * b, GB * b + GB)
                if b:
                    dve.wait_ge(S("sy_mm"), b)
                bc = lambda z, n: z.unsqueeze(2).to_broadcast([P, GB, n, SC])
                bt = lambda z, n: z.unsqueeze(3).to_broadcast([P, GB, n, SC])
                x = t1[:, :].rearrange("p (g t c) -> p g t c", g=GB, c=SC)
                y = t2[:, :].rearrange("p (g t c) -> p g t c", g=GB, c=SC)
                v.tensor_tensor(x, bc(cr_[:, gs], CH + 1), bt(pw_r[:, gs], CH + 1), ALU.mult)
                link(v.tensor_tensor(y, bc(ci_[:, gs], CH + 1), bt(pw_i[:, gs], CH + 1), ALU.mult))
                link(v.tensor_tensor(ca_r[:, :, :, :], x, y, ALU.subtract))
                x = t1[:, 0:512].rearrange("p (g t c) -> p g t c", g=GB, c=SC)
                y = t2[:, 0:512].rearrange("p (g t c) -> p g t c", g=GB, c=SC)
                v.tensor_tensor(x, bt(pv_r[:, gs], CH), bc(br_[:, gs], CH), ALU.mult)
                link(v.tensor_tensor(y, bt(pv_i[:, gs], CH), bc(bi_[:, gs], CH), ALU.mult))
                v.tensor_tensor(ba_r[:, :, :, :], x, y, ALU.subtract).then_inc(S("coef_r"), 1)
                link(v.tensor_copy(r8t[:, :, 1:NCH], cf[:, 3, gs].unsqueeze(2).to_broadcast([P, GB, NCH - 1])))

            def batch_scan(b):
                x = t1[:, 0:512].rearrange("p (g j) -> p g j", g=GB)
                y = t2[:, 0:512].rearrange("p (g j) -> p g j", g=GB)
                zr = ps[:, 6, :].rearrange("p (g j) -> p g j", g=GB)
                zi = ps[:, 7, :].rearrange("p (g j) -> p g j", g=GB)
                dve.wait_ge(S("phi_ready"), b + 1)
                dve.wait_ge(S("z_mm"), b + 1)
                v.tensor_tensor(x, zr, phi_r[:, :, :], ALU.mult)
                link(v.tensor_tensor(y, zi, phi_i[:, :, :], ALU.mult))
                link(v.tensor_tensor(v_r[:, :, :], x, y, ALU.add))
                v.tensor_tensor(x, zi, phi_r[:, :, :], ALU.mult)
                link(v.tensor_tensor(y, zr, phi_i[:, :, :], ALU.mult))
                link(v.tensor_tensor(v_i[:, :, :], x, y, ALU.subtract))
                fl = lambda z: z[:, :, :].rearrange("p g j -> p (g j)")
                v.tensor_tensor_scan(t1[:, 0:512], fl(r8t), fl(v_r), 0.0, ALU.mult, ALU.add)
                ins = v.tensor_tensor_scan(t2[:, 0:512], fl(r8t), fl(v_i), 0.0, ALU.mult, ALU.add)
                ins.then_inc(S("scan_done"), 1)
                dve.wait_ge(S("scan_done"), b + 1)
                v.tensor_tensor(v_r[:, :, :], phi_r[:, :, :], x, ALU.mult)
                link(v.tensor_tensor(v_i[:, :, :], phi_i[:, :, :], y, ALU.mult))
                v.tensor_tensor(xs_r[:, :, 1:NCH], v_r[:, :, 0:NCH - 1], v_i[:, :, 0:NCH - 1], ALU.subtract).then_inc(S("xr_ready"), 1)

            dve.wait_ge(S("par_ld"), 16)
            for k in range(KT):
                dve.wait_ge(S("sq_ready"), k + 1)
                v.tensor_scalar(hT[:, k, :], hT[:, k, :], par[:, O_GMIX + k:O_GMIX + k + 1], None, ALU.mult).then_inc(S("h_ready"), 1)
                if k >= 2:
                    dve.wait_ge(S("sq_added"), k - 1)
                if k:
                    v.tensor_tensor(sqa[:, :], sqa[:, :], sqx[:, k % 2, :], ALU.add).then_inc(S("sq_added"), 1)
            dve.wait_ge(S("sq_mm"), 1)
            for n in range(2):
                v.tensor_scalar(rbc[:, 512 * n:512 * n + 512], ps[:, n, :], 1.0 / D, EPS, ALU.mult, ALU.add)
                ins = v.tensor_scalar(rbh[64 * n:64 * n + 64, :], ps[64 * n:64 * n + 64, n, :], 1.0 / D, EPS, ALU.mult, ALU.add)
            ins.then_inc(S("ms_ready"), 1)
            dve.wait_ge(S("sd_ready"), 1)
            v.reciprocal(rtok[:, :], rtok[:, :]).then_inc(S("rtok_ready"), 1)
            dve.wait_ge(S("sd_ready"), 2)
            link(v.reciprocal(rbh[:, :], rbh[:, :]))
            dve.wait_ge(S("par_ld"), 16)
            dve.wait_ge(S("small_ld"), 80)
            v.tensor_copy(ident_b[:, :], ident)
            dve.wait_ge(S("par_ld"), 16)
            dve.wait_ge(S("small_ld"), 80)
            link(v.tensor_copy(mask_qk[:, :], mask_f[:, :]))
            angles()
            coefficients()
            batch_coef(0)
            for i, un in enumerate(PROJ):
                bank = 2 + i % 4
                if un[0] == "f":
                    if un[1] == 0:
                        dve.wait_ge(S("par_ld"), 16)
                        dve.wait_ge(S("small_ld"), 80)
                        dve.wait_ge(S("pj_mm"), i)
                        link(v.memset(one8[:, :], 1.0))
                    dve.wait_ge(S("pj_mm"), i + 1)
                    zh = zf[:, 512 * un[1]:512 * un[1] + 512]
                    link(v.tensor_tensor(zh, ps[0:8, bank, :], rbh[64 * un[1]:64 * un[1] + 8, :], ALU.mult))
                    v.tensor_scalar(zh, zh, bf[:, 0:1], None, ALU.add).then_inc(S("pj_evac"), 1)
                    if un[1] == 1:
                        dve.wait_ge(S("pj_evac"), i + 1)
                        v.scalar_tensor_tensor(azf[:, :], zf[:, :], -1.0, zf[:, :], ALU.mult, ALU.max).then_inc(S("lf_in"), 1)
                        dve.wait_ge(S("lf_out"), 1)
                        link(v.scalar_tensor_tensor(azf[:, :], zf[:, :], 0.0, azf[:, :], ALU.min, ALU.subtract))
                        link(v.tensor_tensor_scan(zf[:, :], one8[:, :], azf[:, :], 0.0, ALU.mult, ALU.add))
                        v.tensor_scalar(azf[:, :], zf[:, :], -1.0, None, ALU.mult).then_inc(S("cum_ready"), 1)
                if un[0] in "kq":
                    dst = kA if un[0] == "k" else qA
                    m, n = un[1:]
                    if un == ("q", 0, 0):
                        dve.wait_ge(S("c_ld"), 16)
                        dve.wait_ge(S("cq_ld"), 16)
                    dve.wait_ge(S("pj_mm"), i + 1)
                    for half in range(2):
                        ins = v.scalar_tensor_tensor(dst[0:DH, 2 * m + half, 512 * n:512 * n + 512], ps[DH * half:DH * half + DH, bank, :],
                                                     -0.125 if un[0] == "q" else 1.0, rbh[64 * n:64 * n + 64, :], ALU.mult, ALU.mult)
                    ins.then_inc(S("pj_evac"), 1)
                if un == ("k", 3, 1):
                    dve.wait_ge(S("pj_mm"), i + 1)
                    dve.wait_ge(S("c_ld"), 16)
                if i in PIECE_AFTER:
                    kind, b = PIECE_AFTER[i]
                    if kind == "state":
                        batch_scan(b)
                    if kind == "out" and b + 1 < NB:
                        batch_coef(b + 1)

            def row_low(s):
                _, i = TILES[s]
                slot = 2 * (s % 2)
                dve.wait_ge(S("s_mm"), s + 1)
                v.tensor_reduce(low[:, s % 4:s % 4 + 1], ps[:, slot:slot + 2, :].rearrange("p b n -> p (b n)")[:, 0:(i + 1) * P],
                                AX_X, ALU.min).then_inc(S("low_ready"), 1)

            def last_keys(s):
                _, i = TILES[s]
                if i >= 4:
                    dve.wait_ge(S("pb_mm"), LONG[s])
                    if s >= 2:
                        dve.wait_ge(S("pv_mm"), s - 1)
                    v.tensor_copy(probT[:, s % 2, 4:i + 1, :], ps[:, 5, 0:(i - 3) * P].rearrange("p (k q) -> p k q", q=P)).then_inc(S("pb_evac"), 1)

            def head_out(s):
                h, i = TILES[s]
                own = h * (DH + 1) - v_at(h)
                acc = ps[:, 6 + s % 2, own:own + DH + 1]
                dve.wait_ge(S("pv_mm"), s + 1)
                if s >= 2:
                    dve.wait_ge(S("pv_evac"), s - 1)
                link(v.reciprocal(rden[:, s % 2:s % 2 + 1], acc[:, DH:DH + 1]))
                v.tensor_scalar(attn[:, i, DH * h:DH * h + DH], acc[:, 0:DH], rden[:, s % 2:s % 2 + 1], None, ALU.mult).then_inc(S("pv_evac"), 1)

            row_low(0)
            row_low(1)
            for s in range(len(TILES)):
                if s + 2 < len(TILES):
                    row_low(s + 2)
                last_keys(s)
                if s >= 1:
                    head_out(s - 1)
            head_out(len(TILES) - 1)

            dve.wait_ge(S("glu_ld"), 48)
            dve.wait_ge(S("as_ready"), len(TILES))
            link(v.tensor_reduce(ssum[:, :], asq[:, :, :], AX_X, ALU.add))
            v.tensor_scalar(ssum[:, :], ssum[:, :], 1.0 / 512, EPS, ALU.mult, ALU.add).then_inc(S("am_ready"), 1)
            dve.wait_ge(S("ad_ready"), 1)
            link(v.reciprocal(rstd[:, :], ssum[:, :]))
            def add_squares(n):
                co, hf = n // 2, n % 2
                dve.wait_ge(S("ssm_ready"), n + 1)
                if n >= 4:
                    dve.wait_ge(S("sqs_ready"), n - 3)
                half = sqs[:, 0, hf * 512:hf * 512 + 512]
                v.tensor_tensor(half, half, sqs[:, co, hf * 512:hf * 512 + 512], ALU.add).then_inc(S("sqs_ready"), 1)

            for n in range(8):
                co, hf = n // 2, n % 2
                dve.wait_ge(S("gl_sig"), n + 1)
                if n >= 2:
                    dve.wait_ge(S("ssm_ready"), n - 1)
                v.tensor_tensor(osg[:, n % 2, :], gT[:, co, hf * 512:hf * 512 + 512], sgl[:, n % 2, :], ALU.mult).then_inc(S("gl_out"), 1)
                v.scalar_tensor_tensor(attn[:, n, :], attn[:, n, :], rstd[:, n:n + 1], gatt[:, :], ALU.mult, ALU.mult).then_inc(S("an_ready"), 1)
                if n >= 3:
                    add_squares(n - 1)
            add_squares(7)
            dve.wait_ge(S("ss_mm"), 1)
            v.tensor_scalar(rss[:, :], ps[:, 7, 0:8], 1.0 / 512, EPS, ALU.mult, ALU.add).then_inc(S("sm_ready"), 1)
            dve.wait_ge(S("sd2_ready"), 1)
            link(v.reciprocal(rss[:, :], rss[:, :]))

            def resid(t, n):
                w = 2 * t + n
                dve.wait_ge(S("wo_mm"), w + 1)
                xx = x1[:, t, n * 512:n * 512 + 512]
                link(v.scalar_tensor_tensor(xx, ps[:, 2 * (w % 2) + 1, :], rss[:, t:t + 1], xx, ALU.mult, ALU.add))
                v.tensor_tensor(xx, ps[:, 2 * (w % 2), :], xx, ALU.add).then_inc(S("wo_evac"), 1)

            def norm_rows(t):
                dve.wait_ge(S("wo_evac"), 2 * t + 2)
                v.nop().then_inc(S("x1_ready"), 1)
                dve.wait_ge(S("row_sq"), t + 1)
                v.tensor_scalar(ssum[:, t:t + 1], ssum[:, t:t + 1], 1.0 / D, EPS, ALU.mult, ALU.add).then_inc(S("row_ms"), 1)
                dve.wait_ge(S("row_sd"), t + 1)
                link(v.reciprocal(rstd[:, t:t + 1], ssum[:, t:t + 1]))
                v.scalar_tensor_tensor(hn[:, t, :], x1[:, t, :], rstd[:, t:t + 1], gffn[:, :], ALU.mult, ALU.mult).then_inc(S("hn_ready"), 1)

            def logits(t):
                dve.wait_ge(S("rt_mm"), t + 1)
                link(v.tensor_tensor(lg[:, t, :], ps[:, 6 + t % 2, 0:32], brt[:, :], ALU.add))
                link(v.max(m8[:, t, :], lg[:, t, :]))
                v.max_index(i8[:, t, :], m8[:, t, :], lg[:, t, :]).then_inc(S("rt_evac"), 1)
                dve.wait_ge(S("rt_evac"), t + 1)
                ix = idxf[:, TOPK * t:TOPK * t + TOPK]
                link(v.tensor_copy(ix, i8[:, t, 0:TOPK]))
                link(v.tensor_tensor(oh[:, t, :, :], ix.unsqueeze(2).to_broadcast([P, TOPK, 32]),
                                     iota32.unsqueeze(1).to_broadcast([P, TOPK, 32]), ALU.is_equal))
                v.tensor_reduce(sel[:, t, :], oh[:, t, :, :].rearrange("p k e -> p e k"), AX_X, ALU.add).then_inc(S("sel_ready"), 1)

            dve.wait_ge(S("out_ld"), 48)
            dve.wait_ge(S("glu_ld"), 48)
            dve.wait_ge(S("par_ld"), 16)
            dve.wait_ge(S("small_ld"), 80)
            dve.wait_ge(S("gt_mm"), 8)
            for t in range(8):
                resid(t, 0)
                resid(t, 1)
                norm_rows(t)
                if t >= 1:
                    logits(t - 1)
            logits(7)

            v.tensor_tensor(ex4[:, :, :], m8[:, :, 0:TOPK], m8[:, :, 0:1].to_broadcast([P, 8, TOPK]), ALU.subtract).then_inc(S("top_ready"), 1)
            dve.wait_ge(S("sel_ready"), 8)
            dve.wait_ge(S("cnt_mm"), 1)
            R = lambda i: rt[:, i, :]
            tot = ps[:, 0, 256:512].rearrange("p (t e) -> p t e", e=32)
            link(v.memset(prf[:, 0, :], 0.0))
            for t in range(1, 8):
                link(v.tensor_tensor(prf[:, t, :], tot[:, t - 1, :], prf[:, t - 1, :], ALU.add))
            v.tensor_tensor(smap[:, :, :], ps[:, 0, 0:256].rearrange("p (t e) -> p t e", e=32), prf[:, :, :], ALU.add)
            link(v.tensor_tensor(R(0), tot[:, 7, :], prf[:, 7, :], ALU.add))
            link(v.tensor_scalar(R(2), R(0), 0.0, None, ALU.is_gt))
            for i in range(1, T // W):
                link(v.scalar_tensor_tensor(R(2), R(0), float(W * i), R(2), ALU.is_gt, ALU.add))
            link(v.tensor_tensor_scan(R(3), ones[:, 0:32], R(2), 0.0, ALU.mult, ALU.add))
            link(v.tensor_tensor(R(4), R(3), R(2), ALU.subtract))
            link(v.scalar_tensor_tensor(smp[:, :, :], R(4).unsqueeze(1).to_broadcast([P, 8, 32]), float(W), smap[:, :, :], ALU.mult, ALU.add))
            link(v.tensor_tensor(ohp[:, :, :, :], oh[:, :, :, :], smp[:, :, :].unsqueeze(2).to_broadcast([P, 8, TOPK, 32]), ALU.mult))
            link(v.tensor_reduce(psf[:, :], ohp[:, :, :, :].rearrange("p t k e -> p (t k) e"), AX_X, ALU.add))
            link(v.tensor_copy(psi[:, 0, :], psf[:, :]))
            v.tensor_scalar(psi[:, 1, :], psi[:, 0, :], 7, None, ALU.logical_shift_right)
            link(v.tensor_scalar(psi[:, 2, :], psi[:, 0, :], P - 1, None, ALU.bitwise_and))
            link(v.tensor_copy(pcr[:, :, :], psi[:, 1:3, :]))
            nh = 2 * MAXPASS + 4
            for q in range(4):
                c = slice(8 * q, 8 * q + 8)
                v.tensor_tensor(ohr[:, c, :], pcr[:, 1, c].unsqueeze(2).to_broadcast([P, 8, P]), iota.unsqueeze(1).to_broadcast([P, 8, P]), ALU.is_equal)
                link(v.tensor_tensor(ohc[:, c, :], pcr[:, 0, c].unsqueeze(2).to_broadcast([P, 8, nh]),
                                     iota[:, 0:nh].unsqueeze(1).to_broadcast([P, 8, nh]), ALU.is_equal))
                oc = ohc[:, c, :].rearrange("p (t k) c -> p t (k c)", k=TOPK)
                v.tensor_tensor(oc, oc, tid[:, 2 * q:2 * q + 2].unsqueeze(2).to_broadcast([P, 2, TOPK * nh]), ALU.mult).then_inc(S("hot_ready"), 1)
            link(v.tensor_tensor_scan(R(1), ones[:, 0:32], R(0), 0.0, ALU.mult, ALU.add))
            link(v.tensor_tensor(R(1), R(1), R(0), ALU.subtract))
            v.tensor_scalar(R(5), R(4), pidx, None, ALU.is_le)
            link(v.tensor_scalar(R(6), R(3), pidx, None, ALU.is_gt))
            link(v.tensor_tensor(R(5), R(5), R(6), ALU.mult))
            link(v.tensor_scalar(R(6), R(4), pidx, -float(W), ALU.subtract, ALU.mult))
            v.tensor_tensor(R(7), R(1), R(6), ALU.add)
            link(v.tensor_tensor(R(8), R(0), R(6), ALU.subtract))
            v.tensor_tensor(R(7), R(7), R(5), ALU.mult)
            v.tensor_tensor(R(8), R(8), R(5), ALU.mult)
            link(v.tensor_tensor(R(9), iota32, R(5), ALU.mult))
            v.tensor_reduce(tabf[:, 0:1], R(9), AX_X, ALU.add)
            v.tensor_reduce(tabf[:, 1:2], R(7), AX_X, ALU.add)
            link(v.tensor_reduce(tabf[:, 2:3], R(8), AX_X, ALU.add))
            v.tensor_scalar(tabf[:, 2:3], tabf[:, 2:3], float(W), None, ALU.min)
            link(v.tensor_copy(tabf[:, 3:4], R(3)[:, 31:32]))
            v.tensor_copy(passtab[:, :], tabf[:, :]).then_inc(S("tab_ready"), 1)
            dve.wait_ge(S("id_mm"), 1)
            v.tensor_copy(rowid[:, :], ps[:, 1, 0:nh]).then_inc(S("rowid_ready"), 1)
            link(v.tensor_tensor(smap[:, :, :], smap[:, :, :], R(1).unsqueeze(1).to_broadcast([P, 8, 32]), ALU.add))
            link(v.tensor_tensor(oh[:, :, :, :], oh[:, :, :, :], smap[:, :, :].unsqueeze(2).to_broadcast([P, 8, TOPK, 32]), ALU.mult))
            link(v.tensor_reduce(slf[:, :], oh[:, :, :, :].rearrange("p t k e -> p (t k) e"), AX_X, ALU.add))
            v.tensor_copy(slots[:, :], slf[:, :]).then_inc(S("slots_ready"), 1)
            dve.wait_ge(S("ge_ready"), 1)
            link(v.tensor_reduce(sm4[:, :], ex4[:, :, :], AX_X, ALU.add))
            link(v.reciprocal(sm4[:, :], sm4[:, :]))
            link(v.tensor_tensor(gates[:, :, :], ex4[:, :, :], sm4[:, :].unsqueeze(2).to_broadcast([P, 8, TOPK]), ALU.mult))
            dve.wait_ge(S("slots_ready"), 1)

            dve.wait_ge(S("tab_ld"), 16)
            npass = dve.value_load(passrow[0:1, 3:4], min_val=T * TOPK // W, max_val=MAXPASS)
            dve.wait_ge(S("hs_st"), 16 * 8)
            dve.sem_inc(S("gu_evac"), 2)
            v.memset(yT[:, 1, :], 0.0).then_inc(S("yt_evac"), 2)
            with dve.Fori(0, npass) as b:
                dve.wait_ge(S("be_ld"), b * 16 + 16)
                dve.wait_ge(S("yt_evac"), b * KT + 2)
                v.tensor_copy(bcur[:, 0:24], bin_[:, :])
                v.tensor_scalar(bcur[:, 24:32], bin_[:, 8:16], 1.0, None, ALU.add).then_inc(S("be_used"), 1)
                dve.wait_ge(S("be_used"), b + 1)

                def glu_out(f):
                    dve.wait_ge(S("sig_ready"), b * FT + f + 1)
                    v.tensor_tensor(tb[:, f % 2, :], gb[:, f % 2, :], sg[:, f % 2, :], ALU.mult).then_inc(S("tb_ready"), 1)
                    dve.wait_ge(S("tb_ready"), b * FT + f + 1)
                    v.scalar_tensor_tensor(actT[:, f, :], ub[:, f % 2, :], -6.0, tb[:, f % 2, :],
                                           ALU.max, ALU.mult).then_inc(S("act_ready"), 1)

                for f in range(FT):
                    dve.wait_ge(S("gu_mm"), b * FT + f + 1)
                    if f >= 2:
                        dve.wait_ge(S("act_ready"), b * FT + f - 1)
                    v.tensor_scalar(gb[:, f % 2, :], ps[:, f % 2, 0:W], bcur[:, f:f + 1], 7.0, ALU.add, ALU.min).then_inc(S("g_ready"), 1)
                    v.tensor_scalar(ub[:, f % 2, :], ps[:, f % 2, W:2 * W], bcur[:, 24 + f:25 + f], 8.0, ALU.add, ALU.min).then_inc(S("gu_evac"), 1)
                    dve.wait_ge(S("gu_evac"), b * FT + f + 3)
                    glu_out(f)
                for d in range(KT):
                    dve.wait_ge(S("dn_mm"), b * KT + d + 1)
                    dve.wait_ge(S("yt_mm"), b * KT + d + 1)
                    v.tensor_scalar(yT[:, d % 2, :], ps[:, 2 + d % 2, 0:W], bcur[:, 16 + d:17 + d], None, ALU.add).then_inc(S("yt_evac"), 1)

            def combine(t):
                dve.wait_ge(S(f"yg_ld{t % 2}"), 16 * TOPK * (t // 2 + 1))
                for k in range(TOPK):
                    ins = v.scalar_tensor_tensor(x1[:, t, :], yg[:, t % 2, k, :], gates[:, t, k:k + 1], x1[:, t, :], ALU.mult, ALU.add)
                    if k < TOPK - 1:
                        link(ins)
                ins.then_inc(S("x2_ready"), 1)
                dve.wait_ge(S("x2_ready"), t + 1)
                v.nop().then_inc(S("yg_used"), 1)
                dve.wait_ge(S("row_sq"), t + 9)
                v.tensor_scalar(ssum[:, t:t + 1], ssum[:, t:t + 1], 1.0 / D, EPS, ALU.mult, ALU.add).then_inc(S("row_ms"), 1)
                dve.wait_ge(S("row_sd"), t + 9)
                link(v.reciprocal(ssum[:, t:t + 1], ssum[:, t:t + 1]))
                if t >= 2:
                    dve.wait_ge(S("nt_mm"), t - 1)
                v.scalar_tensor_tensor(xn[:, t % 2, :], x1[:, t, :], ssum[:, t:t + 1], grow[:, 0, :], ALU.mult, ALU.mult).then_inc(S("xn_ready"), 1)

            def finish(t):
                for n in range(2):
                    s = slice(n * 512, n * 512 + 512)
                    dve.wait_ge(S("pg_sig"), 2 * t + n + 1)
                    link(v.tensor_tensor(sgp[:, s], ple_in[:, t, s], sgp[:, s], ALU.mult))
                    v.tensor_tensor(x1[:, t, s], x1[:, t, s], sgp[:, s], ALU.add).then_inc(S("x3_half"), 1)
                dve.wait_ge(S("zs_ready"), t + 1)
                v.tensor_scalar(rstd[:, t:t + 1], rstd[:, t:t + 1], 1.0 / D, EPS, ALU.mult, ALU.add).then_inc(S("zm_ready"), 1)
                dve.wait_ge(S("zd_ready"), t + 1)
                link(v.reciprocal(rstd[:, t:t + 1], rstd[:, t:t + 1]))
                if t >= 2:
                    dve.wait_ge(S(f"o_st{t % 2}"), 16 * (t // 2))
                v.scalar_tensor_tensor(ot[:, t % 2, :], x1[:, t, :], rstd[:, t:t + 1], grow[:, 1, :], ALU.mult, ALU.mult).then_inc(S("o_ready"), 1)

            dve.wait_ge(S("wp_ld"), 32)
            combine(0)
            combine(1)
            dve.wait_ge(S("pp_evac"), 16)
            for t in range(8):
                if t + 2 < 8:
                    combine(t + 2)
                finish(t)

        @block.tensor
        def _(pe):
            m = nc.tensor
            pe.wait_ge(S("ones_ready"), 1)
            def piece(kind, b):
                if kind == "prep":
                    if b == 0:
                        pe.wait_ge(S("par_ld"), 16)
                        pe.wait_ge(S("small_ld"), 80)
                        pe.wait_ge(S("pj_evac"), 8)
                        pe.wait_ge(S("rtok_ready"), 1)
                    else:
                        pe.wait_ge(S("sy_evac"), b)
                    for s in range(2 * GB):
                        g = 2 * GB * b + s
                        ins = m.transpose(ps[:, s // 4, (s % 4) * P:(s % 4) * P + P], u[:, g, :, :].rearrange("p t c -> p (t c)"), ident)
                    ins.then_inc(S("ut_mm"), 1)
                    pe.wait_ge(S("coef_r"), b + 1)
                    pe.wait_ge(S("coef_i"), b + 1)
                    for s in range(GB):
                        m.transpose(ps[:, 6, s * P:s * P + P], ba_r[:, s, :, :].rearrange("p t c -> p (t c)"), ident)
                        ins = m.transpose(ps[:, 7, s * P:s * P + P], ba_i[:, s, :, :].rearrange("p t c -> p (t c)"), ident)
                    ins.then_inc(S("bt_mm"), 1)
                    pe.wait_ge(S("ut_evac"), b + 1)
                    for s in range(2 * GB):
                        gp, hf = s // 2, 64 * (s % 2)
                        o_ = ps[0:SC, s % 2, gp * P:gp * P + P]
                        col = GB * b + gp
                        m.matmul(o_, par[hf:hf + 64, O_BR + col * SC:O_BR + col * SC + SC], ca_r[hf:hf + 64, gp, 0:CH, :], start=True, stop=False)
                        ins = m.matmul(o_, par[hf:hf + 64, O_BI + col * SC:O_BI + col * SC + SC], ca_i[hf:hf + 64, gp, 0:CH, :], start=False, stop=True)
                    ins.then_inc(S("kk_mm"), 1)
                elif kind == "state":
                    pe.wait_ge(S("bt_evac"), b + 1)
                    for bank, bm in ((6, bm_r), (7, bm_i)):
                        for s in range(2 * GB):
                            gp, hf = s // 2, 64 * (s % 2)
                            ins = m.matmul(ps[hf:hf + 64, bank, gp * P:gp * P + P], bm[:, gp, hf:hf + 64], ugT[:, s, :], start=True, stop=True)
                    ins.then_inc(S("z_mm"), 1)
                else:
                    pe.wait_ge(S("k_evac"), b + 1)
                    pe.wait_ge(S("tp_ld"), 16 * CH * (b + 1))
                    pe.wait_ge(S("xr_ready"), b + 1)
                    pe.wait_ge(S("xi_ready"), b + 1)
                    for s in range(2 * GB):
                        gp, hf = s // 2, 64 * (s % 2)
                        o_ = ps[:, s % 2, gp * P:gp * P + P]
                        m.matmul(o_, ugT[:, s, :], toep[:, s, :], start=True, stop=False)
                        m.matmul(o_, xs_r[hf:hf + 64, gp, :], ca_r[hf:hf + 64, gp, 1:CH + 1, :], start=False, stop=False)
                        ins = m.matmul(o_, xs_i[hf:hf + 64, gp, :], ca_i[hf:hf + 64, gp, 1:CH + 1, :], start=False, stop=True)
                    ins.then_inc(S("sy_mm"), 1)

            def u_step(t, k):
                return m.matmul(ps[:, 2 + t, :], hT[:, k, t:T:CH], w_u[:, k, :], start=(k == 0), stop=(k == KT - 1))

            pe.wait_ge(S("wu_ld"), 16)
            for k in range(KT // 2):
                pe.wait_ge(S("h_ready"), k + 1)
                for t in range(4):
                    u_step(t, k)
            pe.wait_ge(S("sq_added"), KT - 1)
            for n in range(2):
                ins = m.matmul(ps[:, n, :], ones[:, :], sqa[:, 512 * n:512 * n + 512], start=True, stop=True)
            ins.then_inc(S("sq_mm"), 1)
            pe.wait_ge(S("h_ready"), KT)
            pe.wait_ge(S("wu2_ld"), 16)
            for t in range(4):
                for k in range(KT // 2, KT):
                    ins = u_step(t, k)
                ins.then_inc(S("pj_mm"), 1)
                if t == 1:
                    pe.wait_ge(S("ms_ready"), 1)
                    pe.wait_ge(S("small_ld"), 80)
                    for c in range(16):
                        toks = rbc[:, c:T:CH] if c < 8 else rbc[:, (c - 8) * P:(c - 7) * P]
                        ins = m.matmul(ps[:, 6, c:c + 1], toks, ident[:, 0:1], start=True, stop=True)
                    ins.then_inc(S("rtok_mm"), 1)
            for i, un in enumerate(PROJ):
                if i < 4:
                    continue
                bank = 2 + i % 4
                if i >= 4:
                    pe.wait_ge(S("pj_evac"), i - 3)
                if un[0] == "u":
                    for k in range(KT):
                        ins = m.matmul(ps[:, bank, :], hT[:, k, un[1]:T:CH], w_u[:, k, :], start=(k == 0), stop=(k == KT - 1))
                elif un[0] == "v":
                    if un[1] == 0:
                        pe.wait_ge(S("wv_ld"), 16)
                    for k in range(KT):
                        ins = m.matmul(ps[:, bank, :], hT[:, k, un[1] * P:un[1] * P + P], w_v[:, k, :], start=(k == 0), stop=(k == KT - 1))
                elif un[0] == "f":
                    pe.wait_ge(S("wf_ld"), 16)
                    for k in range(KT):
                        ins = m.matmul(ps[0:8, bank, :], wf[:, k, :], hT[:, k, 512 * un[1]:512 * un[1] + 512], start=(k == 0), stop=(k == KT - 1))
                else:
                    if un[1:] == (0, 0):
                        pe.wait_ge(S(f"w{un[0]}_ld"), 16)
                    w_ = w_k if un[0] == "k" else w_q
                    for k in range(KT):
                        ins = m.matmul(ps[:, bank, :], w_[:, k, un[1] * P:un[1] * P + P], hT[:, k, 512 * un[2]:512 * un[2] + 512],
                                       start=(k == 0), stop=(k == KT - 1))
                ins.then_inc(S("pj_mm"), 1)
                if i in PIECE_AFTER:
                    piece(*PIECE_AFTER[i])

            def scores(s):
                h, i = TILES[s]
                if s >= 2:
                    pe.wait_ge(S("exp_done"), s - 1)
                for c in range((i * P) // 512 + 1):
                    o_ = ps[:, 2 * (s % 2) + c, :]
                    w = min(512, (i + 1) * P - 512 * c)
                    diag = (i * P) // 512 == c
                    ins = m.matmul(o_[:, 0:w], qA[0:66, h, i * P:i * P + P], kA[0:66, h, 512 * c:512 * c + w], start=True, stop=not diag)
                    if diag:
                        ins = m.matmul(o_[:, w - P:w], ident_b[:, :], mask_qk[:, :], start=False, stop=True)
                ins.then_inc(S("s_mm"), 1)

            def turn_probs(s):
                _, i = TILES[s]
                pe.wait_ge(S("exp_done"), s + 1)
                if s:
                    pe.wait_ge(S("pa_evac"), s)
                for k in range(min(i + 1, 4)):
                    ins = m.transpose(ps[:, 4, k * P:k * P + P], probs[:, s % 2, k * P:k * P + P], ident)
                ins.then_inc(S("pa_mm"), 1)
                if i >= 4:
                    if LONG[s] > 1:
                        pe.wait_ge(S("pb_evac"), LONG[s] - 1)
                    for k in range(4, i + 1):
                        ins = m.transpose(ps[:, 5, (k - 4) * P:(k - 4) * P + P], probs[:, s % 2, k * P:k * P + P], ident)
                    ins.then_inc(S("pb_mm"), 1)

            def values(s):
                h, i = TILES[s]
                pe.wait_ge(S("pa_evac"), s + 1)
                if i >= 4:
                    pe.wait_ge(S("pb_evac"), LONG[s])
                if s >= 2:
                    pe.wait_ge(S("pv_evac"), s - 1)
                for k in range(i + 1):
                    ins = m.matmul(ps[:, 6 + s % 2, 0:P], probT[:, s % 2, k, :],
                                   vA[:, k, :, :].rearrange("p h d -> p (h d)")[:, v_at(h):v_at(h) + P], start=(k == 0), stop=(k == i))
                ins.then_inc(S("pv_mm"), 1)

            pe.wait_ge(S("pj_evac"), len(PROJ))
            pe.wait_ge(S("sy_evac"), NB)
            pe.wait_ge(S("aug_q"), 1)
            pe.wait_ge(S("aug_k"), 1)
            pe.wait_ge(S("c_ld"), 16)
            pe.wait_ge(S("cq_ld"), 16)
            scores(0)
            scores(1)
            for s in range(len(TILES)):
                if s + 2 < len(TILES):
                    scores(s + 2)
                turn_probs(s)
                if s >= 1:
                    values(s - 1)
            values(len(TILES) - 1)

            pe.wait_ge(S("gel_out"), 1)
            pe.wait_ge(S("exp_done"), len(TILES))
            for t in range(8):
                if t >= 4:
                    pe.wait_ge(S("gt_evac"), t - 3)
                for c in range(4):
                    ins = m.transpose(ps[:, t % 4, c * P:c * P + P], gtm[:, t, 8 * c:8 * c + 8, :].rearrange("p g c -> p (g c)"), ident)
                ins.then_inc(S("gt_mm"), 1)
            pe.wait_ge(S("gt_evac"), 8)
            pe.wait_ge(S("glu_ld"), 48)
            pe.wait_ge(S("pv_evac"), len(TILES))
            for n in range(8):
                co, hf = n // 2, n % 2
                if n >= 2:
                    pe.wait_ge(S("gl_sig"), n - 1)
                for k in range(4):
                    ins = m.matmul(ps[:, 4 + n % 2, :], wglu[:, k, co * P:co * P + P], gT[:, k, hf * 512:hf * 512 + 512],
                                   start=(k == 0), stop=(k == 3))
                ins.then_inc(S("gl_mm"), 1)
            for i in range(QT):
                pe.wait_ge(S("an_ready"), i + 1)
                if i >= 4:
                    pe.wait_ge(S("at_evac"), i - 3)
                for c in range(4):
                    ins = m.transpose(ps[:, i % 4, c * P:c * P + P], attn[:, i, c * P:c * P + P], ident)
                ins.then_inc(S("at_mm"), 1)

            pe.wait_ge(S("ssm_ready"), 8)
            pe.wait_ge(S("sqs_ready"), 6)
            for t in range(8):
                ins = m.matmul(ps[:, 7, t:t + 1], sqs[:, 0, t * P:t * P + P], ones[:, 0:1], start=True, stop=True)
            ins.then_inc(S("ss_mm"), 1)
            def project(t, n):
                w = 2 * t + n
                if w >= 2:
                    pe.wait_ge(S("wo_evac"), w - 1)
                for k in range(4):
                    m.matmul(ps[:, 2 * (w % 2), :], attnT[:, k, t:T:CH], wout[:, k, n * 512:n * 512 + 512], start=(k == 0), stop=(k == 3))
                for k in range(4):
                    ins = m.matmul(ps[:, 2 * (w % 2) + 1, :], ssmT[:, k, t * P:t * P + P], wout[:, 4 + k, n * 512:n * 512 + 512],
                                   start=(k == 0), stop=(k == 3))
                ins.then_inc(S("wo_mm"), 1)

            def turn_rows(t):
                pe.wait_ge(S("hn_ready"), t + 1)
                if t:
                    pe.wait_ge(S("ht_evac"), t)
                for k in range(KT):
                    ins = m.transpose(ps[:, 4 + k // 4, (k % 4) * P:(k % 4) * P + P], hn[:, t, k * P:k * P + P], ident)
                ins.then_inc(S("ht_mm"), 1)

            def route(t):
                pe.wait_ge(S("ht_evac"), t + 1)
                if t >= 2:
                    pe.wait_ge(S("rt_evac"), t - 1)
                for k in range(KT):
                    ins = m.matmul(ps[:, 6 + t % 2, 0:32], h2T[:, t % 2, k, :], wr[:, k, :], start=(k == 0), stop=(k == KT - 1))
                ins.then_inc(S("rt_mm"), 1)

            pe.wait_ge(S("at_evac"), QT)
            pe.wait_ge(S("out_ld"), 48)
            pe.wait_ge(S("sm_ready"), 1)
            project(0, 0)
            project(0, 1)
            for t in range(8):
                if t + 1 < 8:
                    project(t + 1, 0)
                turn_rows(t)
                if t + 1 < 8:
                    project(t + 1, 1)
                route(t)
            pe.wait_ge(S("sel_ready"), 8)
            pe.wait_ge(S("wo_evac"), 16)
            sf = sel[:, :, :].rearrange("p t e -> p (t e)")
            m.matmul(ps[:, 0, 0:256], tri, sf, start=True, stop=True)
            m.matmul(ps[:, 0, 256:512], ones[:, :], sf, start=True, stop=True).then_inc(S("cnt_mm"), 1)
            for q in range(4):
                pe.wait_ge(S("hot_ready"), q + 1)
                for c in range(8 * q, 8 * q + 8):
                    ins = m.matmul(ps[:, 1, 0:2 * MAXPASS + 4], ohr[:, c, :], ohc[:, c, :], start=(c == 0), stop=(c == 31))
            ins.then_inc(S("id_mm"), 1)

            pe.wait_ge(S("tab_ld"), 16)
            npass = pe.value_load(passrow[0:1, 3:4], min_val=T * TOPK // W, max_val=MAXPASS)
            def turn_half(a_):
                for j in range(2):
                    for q in range(4):
                        k = 4 * j + q
                        ins = m.transpose(ps[:, 6 - 2 * a_ + j, q * P:q * P + P], xg[:, a_, k * P:k * P + P], ident)
                    ins.then_inc(S("xp2_mm" if a_ else "xp_mm"), 1)

            def turn_rows_in(n):
                turn_half(0)
                with pe.If_lt(n, P + 1):
                    pe.sem_inc(S("xp2_mm"), 2)
                with pe.Else():
                    turn_half(1)

            pe.wait_ge(S("rows0_ld"), 16)
            pe.wait_ge(S("rows1_ld"), 16)
            n = pe.alloc_register("n_rows")
            n_next = pe.alloc_register("n_rows_next")
            pe.reg_load(n, passrow[0:1, 2:3])
            turn_rows_in(n)
            pe.sem_inc(S("yt_mm"), 1)

            def by_width(n, body):
                def level(lo, hi):
                    if lo + 1 == hi:
                        body(WIDTHS[lo])
                        return
                    mid = (lo + hi) // 2
                    with pe.If_lt(n, WIDTHS[mid - 1] + 1):
                        level(lo, mid)
                        pe.nop()
                    with pe.Else():
                        level(mid, hi)
                        pe.nop()
                with pe.If_lt(n, WIDTHS[0] + 1):
                    body(WIDTHS[0])
                with pe.Else():
                    level(1, len(WIDTHS))
                    pe.nop()

            def turn_y(d, halves, ready, free):
                pe.wait_ge(S("yt_evac"), ready)
                pe.wait_ge(S("y_evac"), free)
                for a_ in range(halves):
                    ins = m.transpose(ps[:, 4 + d % 2, a_ * P:a_ * P + P], yT[:, d % 2, a_ * P:a_ * P + P], ident)
                ins.then_inc(S("yt_mm"), 1)

            with pe.Fori(0, npass) as b:
                pe.wait_ge(S("xt_evac"), b * 2 + 2)
                pe.wait_ge(S("xt2_evac"), b * 2 + 2)

                def gate_up(w):
                    for f in range(FT):
                        pe.wait_ge(S(f"in_ld{f}"), b * 16 + 32)
                        pe.wait_ge(S("gu_evac"), b * FT + f + 1)
                        for g_ in range(2):
                            for k in range(KT):
                                ins = m.matmul(ps[:, f % 2, g_ * W:g_ * W + w], wg[:, f, k, g_, :], xT[:, k, 0:w], start=(k == 0), stop=(k == KT - 1))
                        ins.then_inc(S("gu_mm"), 1)
                        if f == 0:
                            turn_y(KT - 1, 2, b * KT + 2, b * KT + 1)

                by_width(n, gate_up)
                pe.wait_ge(S("rows0_ld"), b * 16 + 32)
                pe.wait_ge(S("rows1_ld"), b * 16 + 32)
                pe.reg_load(n_next, passrow[0:1, bass.ds(4 * b + 6, 1)])
                pe.wait_ge(S("y_evac"), b * KT + 3)
                turn_rows_in(n_next)

                def down(w):
                    for d in range(KT):
                        if d % 2 == 0:
                            pe.wait_ge(S(f"dn_ld{d // 2}"), b * 16 + 16)
                        pe.wait_ge(S("yt_evac"), b * KT + d + 1)
                        for f in range(FT):
                            if d == 0:
                                pe.wait_ge(S("act_ready"), b * FT + f + 1)
                            ins = m.matmul(ps[:, 2 + d % 2, 0:w], wd[:, d, f, :], actT[:, f, 0:w], start=(f == 0), stop=(f == FT - 1))
                        ins.then_inc(S("dn_mm"), 1)
                        if d in (1, 2):
                            pe.wait_ge(S("xt2_evac"), b * 2 + d + 2)
                        if d >= 1:
                            turn_y(d - 1, 1 if w <= P else 2, b * KT + d + 2, b * KT + d + 1)

                by_width(n, down)
                pe.reg_mov(n, n_next)
            turn_y(KT - 1, 2, npass * KT + 2, npass * KT + 1)

            pe.wait_ge(S("wpp_ld"), 32)
            pe.wait_ge(S("y_evac"), npass * KT + 3)
            for i in range(16):
                if i >= 4:
                    pe.wait_ge(S("pp_evac"), i - 3)
                for k in range(2):
                    ins = m.matmul(ps[:, 4 + i % 4, :], ppT[:, k, i // 2, :], wpp[:, k, 512 * (i % 2):512 * (i % 2) + 512], start=(k == 0), stop=(k == 1))
                ins.then_inc(S("pp_mm"), 1)

            def turn_tail(t):
                pe.wait_ge(S("xn_ready"), t + 1)
                if t:
                    pe.wait_ge(S("nt_evac"), t)
                for k in range(KT):
                    ins = m.transpose(ps[:, k // 4, (k % 4) * P:(k % 4) * P + P], xn[:, t % 2, k * P:k * P + P], ident)
                ins.then_inc(S("nt_mm"), 1)

            def gate(t, n):
                if n == 0:
                    pe.wait_ge(S("nt_evac"), t + 1)
                if t:
                    pe.wait_ge(S("pg_sig"), 2 * t + n - 1)
                for k in range(KT):
                    ins = m.matmul(ps[:, 2 + n, :], xnT[:, t % 2, k, :], wpg[:, k, n * 512:n * 512 + 512], start=(k == 0), stop=(k == KT - 1))
                ins.then_inc(S("pg_mm"), 1)

            pe.wait_ge(S("wp_ld"), 32)
            turn_tail(0)
            for t in range(8):
                gate(t, 0)
                if t + 1 < 8:
                    turn_tail(t + 1)
                gate(t, 1)


def shape_constants():
    c = np.zeros((P, N_CONST), np.float32)
    i = np.arange(P)
    c[:, O_ID:O_ID + P] = np.eye(P, dtype=np.float32)
    c[:, O_TRI:O_TRI + P] = (i[:, None] < i[None, :])
    c[:, O_MA:O_MA + P] = np.where(i[None, :] <= i[:, None], 0.0, FAR)
    c[:, O_IOTA:O_IOTA + P] = np.arange(P)
    c[:, O_TID:O_TID + 8] = i[:, None] + P * np.arange(8)
    c[:, O_PIDX] = i
    return c


def kernel(x, p, norm_mix_g, w_in, b_f, lam_re, lam_im, log_dt, b_re, b_im, c_re, c_im, d_skip, w_glu, b_glu,
           attn_out_g, ssm_out_g, w_out, norm_ffn_g, w_router, b_router, w_gu, b_gu, w_dn, b_dn,
           norm_ple_g, w_ple_gate, w_ple_proj, norm_final_g):
    import concourse.bacc as bacc
    from concourse.bass_utils import run_bass_kernel_spmd

    A = np.asarray
    cont = np.ascontiguousarray

    def col(a):
        return A(a).reshape(-1, P).T

    def kmaj(a):
        a = A(a)
        return cont(a.reshape(-1, P, a.shape[-1]).transpose(1, 0, 2))

    def pairs(a):
        a = A(a)
        a = a.reshape((GP, 2, 64) + a.shape[2:])
        return np.moveaxis(a, 0, 2).reshape(P, -1)

    small = np.concatenate([
        col(norm_mix_g[0]), col(ssm_out_g[0]), col(b_glu[0]),
        pairs(lam_re[0]), pairs(lam_im[0]), pairs(np.broadcast_to(A(log_dt[0])[:, None], (NG, 64))),
        pairs(b_re[0]), pairs(b_im[0]), pairs(A(c_re[0]).transpose(0, 2, 1)), pairs(A(c_im[0]).transpose(0, 2, 1))], axis=1)
    x2 = A(x).reshape(T, D)
    gu = A(w_gu).reshape(E, KT, P, 2, FT, P).transpose(0, 4, 2, 1, 3, 5)
    dn = A(w_dn).reshape(E, FT, P, KT // 2, 2, P).transpose(0, 3, 2, 4, 1, 5)
    bgu = A(b_gu).reshape(E, 16, P).transpose(0, 2, 1)
    bdn = A(b_dn).reshape(E, 8, P).transpose(0, 2, 1)
    ple = A(p).reshape(NCH, CH, 2, P).transpose(3, 2, 1, 0)
    ins = {
        "x_cm": kmaj(x2.T), "x_tm": x2.reshape(P, 8, D), "pT": ple, "small": small, "consts": shape_constants(),
        "b_f": A(b_f).reshape(8, 1), "d_skipT": A(d_skip).reshape(NG, SC).T,
        "b_router": np.broadcast_to(A(b_router).reshape(1, E), (P, E)),
        "gains": np.broadcast_to(np.concatenate([A(norm_ffn_g[0]), A(norm_ple_g[0]), A(norm_final_g), A(attn_out_g[0])]), (P, 3 * D + 512)),
        "w_in": kmaj(w_in[0]), "w_glu": kmaj(w_glu[0]), "w_out": kmaj(w_out[0]), "w_router": kmaj(w_router[0]),
        "w_gu": gu, "w_dn": dn, "b_exp": np.concatenate([bgu, bdn], axis=2),
        "w_ple_gate": kmaj(w_ple_gate[0]), "w_ple_proj": kmaj(w_ple_proj[0]),
    }
    nc = bacc.Bacc("TRN2", target_bir_lowering=False, num_devices=1)
    arrays, aps = {}, []
    for name, a in ins.items():
        arrays[f"in_{name}"] = cont(a)
        aps.append(nc.dram_tensor(f"in_{name}", a.shape, mybir.dt.from_np(a.dtype), kind="ExternalInput").ap())
    out = nc.dram_tensor("out", (P, 8, D), F32, kind="ExternalOutput").ap()
    hs = nc.dram_tensor("normalised_rows", (T, D), F32).ap()
    ys = nc.dram_tensor("expert_rows", (ROWS + W, D), F32).ap()
    build(nc, *aps, out, hs, ys)
    r = run_bass_kernel_spmd(nc, [arrays], core_ids=[0])
    return r.results[0]["out"].reshape(1, T, D)
```
